# Optimizing a Trainium2 kernel written in Bass

```python
import jax, jax.numpy as jnp
from jax import lax
import numpy as np
import math

D_MODEL = 1024
BATCH = 1
SEQ = 256
DEPTH = 4

N_MIXERS = 3
HEAD_DIM = 64
RMS_EPS = 1e-6

NSA_HEADS = 16
NSA_GROUPS = 4
NSA_REP = NSA_HEADS // NSA_GROUPS
NSA_KV = NSA_GROUPS * HEAD_DIM
CMP_BLOCK = 32
CMP_STRIDE = 16
CMP_HIDDEN = 256
SLC_BLOCK = 64
SLC_TOPK = 16
WINDOW = 512
WIN_QBLOCK = 128
NSA_Q_CHUNK = 64
NSA_IN = NSA_HEADS * HEAD_DIM + 6 * NSA_KV + 3 * NSA_HEADS
NSA_SPLITS = [NSA_HEADS * HEAD_DIM + i * NSA_KV for i in range(7)]

MOBA_HEADS = 16
MOBA_BLOCK = 256
MOBA_TOPK = 3
MOBA_Q_CHUNK = 32

CONV_WIDTH = 3

D_FF = -(-8 * D_MODEL // (3 * 256)) * 256


def rms_norm(x, g):
    xf = x.astype(jnp.float32)
    y = xf * lax.rsqrt(jnp.mean(xf * xf, axis=-1, keepdims=True) + RMS_EPS)
    return (y * g.astype(jnp.float32)).astype(x.dtype)

def masked_softmax(s, mask):
    s = jnp.where(mask, s.astype(jnp.float32), -jnp.inf)
    m = jnp.max(s, axis=-1, keepdims=True)
    m = jnp.where(jnp.isfinite(m), m, 0.0)
    e = jnp.where(mask, jnp.exp(s - m), 0.0)
    d = jnp.sum(e, axis=-1, keepdims=True)
    return e / jnp.where(d > 0, d, 1.0)

def gather_blocks(blocks, idx):
    return jax.vmap(jax.vmap(lambda b, i: b[i]))(blocks, idx)

def swiglu(a, w_gate, w_up, w_down):
    return (jax.nn.silu(a @ w_gate) * (a @ w_up)) @ w_down

def nsa_mixer(h, w_in, w_out, pos_k, pos_v, k_w1, k_w2, v_w1, v_w2):
    B_, S_, _ = h.shape
    G, R, dh = NSA_GROUPS, NSA_REP, HEAD_DIM
    q, k_c, v_c, k_s, v_s, k_w, v_w, gates = jnp.split(h @ w_in, NSA_SPLITS, axis=-1)
    q = q.reshape(B_, S_, G, R, dh) * (HEAD_DIM ** -0.5)
    kvs = [a.reshape(B_, S_, G, dh) for a in (k_c, v_c, k_s, v_s, k_w, v_w)]
    k_c, v_c, k_s, v_s, k_w, v_w = kvs
    gates = jax.nn.sigmoid(gates.astype(jnp.float32)).reshape(B_, S_, 3, G, R)
    t = jnp.arange(S_)

    n_cmp = (S_ - CMP_BLOCK) // CMP_STRIDE + 1
    cmp_idx = jnp.arange(n_cmp)[:, None] * CMP_STRIDE + jnp.arange(CMP_BLOCK)[None, :]

    def compress(kv, pos, w1, w2):
        blk = kv[:, cmp_idx] + pos[None, None, :, None, :]
        blk = jnp.moveaxis(blk, 3, 2).reshape(B_, n_cmp, G, CMP_BLOCK * dh)
        return jax.nn.gelu(blk @ w1) @ w2

    kc = compress(k_c, pos_k, k_w1, k_w2)
    vc = compress(v_c, pos_v, v_w1, v_w2)
    cmp_end = jnp.arange(n_cmp) * CMP_STRIDE + CMP_BLOCK - 1
    cmp_mask = cmp_end[None, :] <= t[:, None]
    s_cmp = jnp.einsum('bsgrd,bcgd->bgrsc', q, kc)
    p_cmp = masked_softmax(s_cmp, cmp_mask)
    o_cmp = jnp.einsum('bgrsc,bcgd->bsgrd', p_cmp.astype(vc.dtype), vc)

    n_slc = S_ // SLC_BLOCK
    c_start = jnp.arange(n_cmp) * CMP_STRIDE
    j_start = jnp.arange(n_slc) * SLC_BLOCK
    overlap = ((c_start[:, None] < j_start[None, :] + SLC_BLOCK)
               & (c_start[:, None] + CMP_BLOCK > j_start[None, :])).astype(jnp.float32)
    imp = jnp.einsum('bgrsc,cn->bgsn', p_cmp, overlap)
    cur = t // SLC_BLOCK
    blk_ids = jnp.arange(n_slc)
    forced = ((blk_ids[None, :] == 0) | (blk_ids[None, :] == cur[:, None])
              | (blk_ids[None, :] == cur[:, None] - 1))
    imp = jnp.where(forced, jnp.inf,
                    jnp.where(blk_ids[None, :] <= cur[:, None], imp, -jnp.inf))
    n_sel = min(SLC_TOPK, n_slc)
    _, sel = lax.top_k(imp, n_sel)

    kb = k_s.reshape(B_, n_slc, SLC_BLOCK, G, dh).transpose(0, 3, 1, 2, 4)
    vb = v_s.reshape(B_, n_slc, SLC_BLOCK, G, dh).transpose(0, 3, 1, 2, 4)
    Qc = NSA_Q_CHUNK
    n_qc = S_ // Qc
    q_chunks = q.reshape(B_, n_qc, Qc, G, R, dh).transpose(1, 0, 2, 3, 4, 5)
    sel_chunks = sel.reshape(B_, G, n_qc, Qc, n_sel).transpose(2, 0, 1, 3, 4)

    def slc_chunk(args):
        ci, qc, ix = args
        tq = ci * Qc + jnp.arange(Qc)
        kg = gather_blocks(kb, ix)
        vg = gather_blocks(vb, ix)
        kpos = ix[..., None] * SLC_BLOCK + jnp.arange(SLC_BLOCK)
        mask = (kpos <= tq[:, None, None]).reshape(B_, G, Qc, n_sel * SLC_BLOCK)[:, :, None]
        s = jnp.einsum('bqgrd,bgqnkd->bgrqnk', qc, kg).reshape(B_, G, R, Qc, n_sel * SLC_BLOCK)
        p = masked_softmax(s, mask).reshape(B_, G, R, Qc, n_sel, SLC_BLOCK)
        return jnp.einsum('bgrqnk,bgqnkd->bqgrd', p.astype(vg.dtype), vg)

    o_slc = lax.map(slc_chunk, (jnp.arange(n_qc), q_chunks, sel_chunks))
    o_slc = o_slc.transpose(1, 0, 2, 3, 4, 5).reshape(B_, S_, G, R, dh)

    QB = WIN_QBLOCK
    nqb = S_ // QB
    n_back = WINDOW // QB
    pad = n_back * QB

    def band(kv):
        kp = jnp.pad(kv, ((0, 0), (pad, 0), (0, 0), (0, 0))).reshape(B_, nqb + n_back, QB, G, dh)
        return jnp.concatenate([kp[:, i:i + nqb] for i in range(n_back + 1)], axis=2)

    kwb = band(k_w)
    vwb = band(v_w)
    qb = q.reshape(B_, nqb, QB, G, R, dh)
    qpos = t.reshape(nqb, QB)
    kpos = (jnp.arange(nqb)[:, None] - n_back) * QB + jnp.arange((n_back + 1) * QB)[None, :]
    wmask = ((kpos[:, None, :] <= qpos[:, :, None])
             & (kpos[:, None, :] > qpos[:, :, None] - WINDOW)
             & (kpos[:, None, :] >= 0))
    s_win = jnp.einsum('bnqgrd,bnkgd->bgrnqk', qb, kwb)
    p_win = masked_softmax(s_win, wmask)
    o_win = jnp.einsum('bgrnqk,bnkgd->bnqgrd', p_win.astype(vwb.dtype), vwb).reshape(B_, S_, G, R, dh)

    o = (gates[:, :, 0, :, :, None] * o_cmp + gates[:, :, 1, :, :, None] * o_slc
         + gates[:, :, 2, :, :, None] * o_win).astype(h.dtype)
    return o.reshape(B_, S_, NSA_HEADS * dh) @ w_out

def moba_mixer(h, w_in, w_out):
    B_, S_, _ = h.shape
    H, dh = MOBA_HEADS, HEAD_DIM
    q, k, v = jnp.split(h @ w_in, 3, axis=-1)
    n_blk = -(-S_ // MOBA_BLOCK)
    S_pad = n_blk * MOBA_BLOCK

    def heads(a):
        a = jnp.pad(a, ((0, 0), (0, S_pad - S_), (0, 0)))
        return a.reshape(B_, S_pad, H, dh).transpose(0, 2, 1, 3)

    q = heads(q) * (HEAD_DIM ** -0.5)
    k = heads(k)
    v = heads(v)
    kb = k.reshape(B_, H, n_blk, MOBA_BLOCK, dh)
    vb = v.reshape(B_, H, n_blk, MOBA_BLOCK, dh)
    k_mean = jnp.mean(kb.astype(jnp.float32), axis=3)
    t = jnp.arange(S_pad)
    cur = t // MOBA_BLOCK
    n_sel = min(MOBA_TOPK, n_blk - 1)
    if n_sel > 0:
        score = jnp.einsum('bhsd,bhnd->bhsn', q.astype(jnp.float32), k_mean)
        past = jnp.arange(n_blk)[None, :] < cur[:, None]
        _, sel = lax.top_k(jnp.where(past, score, -jnp.inf), n_sel)
    else:
        sel = jnp.zeros((B_, H, S_pad, 0), jnp.int32)
    Qc = MOBA_Q_CHUNK
    n_qc = S_pad // Qc
    q_chunks = q.reshape(B_, H, n_qc, Qc, dh).transpose(2, 0, 1, 3, 4)
    sel_chunks = sel.reshape(B_, H, n_qc, Qc, n_sel).transpose(2, 0, 1, 3, 4)

    def chunk(args):
        ci, qc, ix = args
        tq = ci * Qc + jnp.arange(Qc)
        own = (ci * Qc) // MOBA_BLOCK
        k_own = lax.dynamic_index_in_dim(kb, own, axis=2, keepdims=False)
        v_own = lax.dynamic_index_in_dim(vb, own, axis=2, keepdims=False)
        own_pos = own * MOBA_BLOCK + jnp.arange(MOBA_BLOCK)
        m_own = jnp.broadcast_to(own_pos[None, :] <= tq[:, None], (B_, H, Qc, MOBA_BLOCK))
        s_own = jnp.einsum('bhqd,bhkd->bhqk', qc, k_own)
        if n_sel == 0:
            p = masked_softmax(s_own, m_own)
            return jnp.einsum('bhqk,bhkd->bhqd', p.astype(v_own.dtype), v_own)
        kg = gather_blocks(kb, ix)
        vg = gather_blocks(vb, ix)
        n_keys = n_sel * MOBA_BLOCK
        s_sel = jnp.einsum('bhqd,bhqnkd->bhqnk', qc, kg).reshape(B_, H, Qc, n_keys)
        valid = ix < own
        m_sel = jnp.broadcast_to(valid[..., None], (B_, H, Qc, n_sel, MOBA_BLOCK)).reshape(B_, H, Qc, n_keys)
        p = masked_softmax(jnp.concatenate([s_sel, s_own], axis=-1),
                           jnp.concatenate([m_sel, m_own], axis=-1))
        p_sel = p[..., :n_keys].reshape(B_, H, Qc, n_sel, MOBA_BLOCK).astype(vg.dtype)
        p_own = p[..., n_keys:].astype(v_own.dtype)
        return (jnp.einsum('bhqnk,bhqnkd->bhqd', p_sel, vg)
                + jnp.einsum('bhqk,bhkd->bhqd', p_own, v_own))

    o = lax.map(chunk, (jnp.arange(n_qc), q_chunks, sel_chunks))
    o = o.transpose(1, 2, 0, 3, 4).reshape(B_, H, S_pad, dh)[:, :, :S_]
    o = o.transpose(0, 2, 1, 3).reshape(B_, S_, H * dh)
    return o @ w_out

def short_conv_mixer(h, w_in, conv_w, w_out):
    d = h.shape[-1]
    b_gate, c_gate, u = jnp.split(h @ w_in, 3, axis=-1)
    z = c_gate * u
    y = lax.conv_general_dilated(
        z, conv_w[:, None, :].astype(z.dtype), window_strides=(1,),
        padding=[(CONV_WIDTH - 1, 0)],
        dimension_numbers=('NWC', 'WIO', 'NWC'), feature_group_count=d)
    return (b_gate * y) @ w_out

def first_inputs(seed: int = 0) -> dict:
    key = jax.random.key(seed)
    ks = jax.random.split(key, 20)
    f32 = jnp.float32
    n_a = (DEPTH + 2) // 3
    n_b = (DEPTH + 1) // 3
    n_c = DEPTH // 3

    def w(k, shape, fan_in):
        return jax.random.normal(k, shape, f32) * (fan_in ** -0.5)

    def gain(k, shape):
        return 1.0 + 0.02 * jax.random.normal(k, shape, f32)

    return {
        "x": jax.random.normal(ks[0], (BATCH, SEQ, D_MODEL), f32),
        "norm_mix": gain(ks[1], (DEPTH, D_MODEL)),
        "norm_ffn": gain(ks[2], (DEPTH, D_MODEL)),
        "norm_final": gain(ks[3], (D_MODEL,)),
        "ffn_w_gate": w(ks[4], (DEPTH, D_MODEL, D_FF), D_MODEL),
        "ffn_w_up": w(ks[5], (DEPTH, D_MODEL, D_FF), D_MODEL),
        "ffn_w_down": w(ks[6], (DEPTH, D_FF, D_MODEL), D_FF),
        "nsa_w_in": w(ks[7], (n_a, D_MODEL, NSA_IN), D_MODEL),
        "nsa_w_out": w(ks[8], (n_a, NSA_HEADS * HEAD_DIM, D_MODEL), NSA_HEADS * HEAD_DIM),
        "nsa_cmp_pos_k": 0.1 * jax.random.normal(ks[9], (n_a, CMP_BLOCK, HEAD_DIM), f32),
        "nsa_cmp_pos_v": 0.1 * jax.random.normal(ks[10], (n_a, CMP_BLOCK, HEAD_DIM), f32),
        "nsa_cmp_k_w1": w(ks[11], (n_a, CMP_BLOCK * HEAD_DIM, CMP_HIDDEN), CMP_BLOCK * HEAD_DIM),
        "nsa_cmp_k_w2": w(ks[12], (n_a, CMP_HIDDEN, HEAD_DIM), CMP_HIDDEN),
        "nsa_cmp_v_w1": w(ks[13], (n_a, CMP_BLOCK * HEAD_DIM, CMP_HIDDEN), CMP_BLOCK * HEAD_DIM),
        "nsa_cmp_v_w2": w(ks[14], (n_a, CMP_HIDDEN, HEAD_DIM), CMP_HIDDEN),
        "moba_w_in": w(ks[15], (n_b, D_MODEL, 3 * MOBA_HEADS * HEAD_DIM), D_MODEL),
        "moba_w_out": w(ks[16], (n_b, MOBA_HEADS * HEAD_DIM, D_MODEL), MOBA_HEADS * HEAD_DIM),
        "conv_w_in": w(ks[17], (n_c, D_MODEL, 3 * D_MODEL), D_MODEL),
        "conv_w": w(ks[18], (n_c, CONV_WIDTH, D_MODEL), CONV_WIDTH),
        "conv_w_out": w(ks[19], (n_c, D_MODEL, D_MODEL), D_MODEL),
    }

def first_block(x, norm_mix, norm_ffn, norm_final, ffn_w_gate, ffn_w_up, ffn_w_down,
              nsa_w_in, nsa_w_out, nsa_cmp_pos_k, nsa_cmp_pos_v, nsa_cmp_k_w1,
              nsa_cmp_k_w2, nsa_cmp_v_w1, nsa_cmp_v_w2, moba_w_in, moba_w_out,
              conv_w_in, conv_w, conv_w_out):
    h = x
    for i in range(DEPTH):
        kind, j = i % N_MIXERS, i // N_MIXERS
        a = rms_norm(h, norm_mix[i])
        if kind == 0:
            m = nsa_mixer(a, nsa_w_in[j], nsa_w_out[j], nsa_cmp_pos_k[j], nsa_cmp_pos_v[j],
                          nsa_cmp_k_w1[j], nsa_cmp_k_w2[j], nsa_cmp_v_w1[j], nsa_cmp_v_w2[j])
        elif kind == 1:
            m = moba_mixer(a, moba_w_in[j], moba_w_out[j])
        else:
            m = short_conv_mixer(a, conv_w_in[j], conv_w[j], conv_w_out[j])
        h = h + m
        a = rms_norm(h, norm_ffn[i])
        h = h + swiglu(a, ffn_w_gate[i], ffn_w_up[i], ffn_w_down[i])
    return rms_norm(h, norm_final)


DEPTH_2 = 2

GRID_W = 64
CTX_LEN = 256
Q_BLOCK = 128
ROPE_THETA = 10000.0
LN_EPS = 1e-5
D_FF_2 = 4 * D_MODEL

MLA_HEADS = 8
MLA_Q_RANK = 512
MLA_KV_RANK = 256
MLA_NOPE = 128
MLA_ROPE = 64
MLA_V = 128

NA_HEADS = 16
NA_HEAD_DIM = D_MODEL // NA_HEADS
NA_WIN_ROWS = 8
NA_WIN_COLS = 16

GQA_HEAD_DIM = 128
GQA_Q_HEADS = D_MODEL // GQA_HEAD_DIM
GQA_KV_HEADS = GQA_Q_HEADS // 4
GQA_GROUP = GQA_Q_HEADS // GQA_KV_HEADS


def _layer_norm(x, g, b):
    xf = x.astype(jnp.float32)
    mu = jnp.mean(xf, -1, keepdims=True)
    var = jnp.mean(jnp.square(xf - mu), -1, keepdims=True)
    return ((xf - mu) * lax.rsqrt(var + LN_EPS) * g + b).astype(x.dtype)

def _rms_norm(x, g):
    xf = x.astype(jnp.float32)
    return (xf * lax.rsqrt(jnp.mean(xf * xf, -1, keepdims=True) + RMS_EPS) * g).astype(x.dtype)

def _rope_1d(x, pos):
    half = x.shape[-1] // 2
    freqs = ROPE_THETA ** (-jnp.arange(half, dtype=jnp.float32) / half)
    ang = pos.astype(jnp.float32)[:, None, None] * freqs
    cos, sin = jnp.cos(ang), jnp.sin(ang)
    xf = x.astype(jnp.float32)
    x1, x2 = xf[..., :half], xf[..., half:]
    return jnp.concatenate([x1 * cos - x2 * sin, x1 * sin + x2 * cos], -1).astype(x.dtype)

def _rope_2d(x, rows, cols):
    h = x.shape[-1] // 2
    return jnp.concatenate([_rope_1d(x[..., :h], rows), _rope_1d(x[..., h:], cols)], -1)

def _grid_positions(s):
    t = jnp.arange(s, dtype=jnp.int32)
    return t // GRID_W, t % GRID_W

def _block_attention(q, k, v, scale):
    b, sq, hk, g, dk = q.shape
    nb = sq // Q_BLOCK
    qb = q.reshape(b, nb, Q_BLOCK, hk, g, dk).transpose(1, 0, 2, 3, 4, 5)

    def step(qi):
        s = jnp.einsum('bqhgd,bkhd->bhgqk', qi, k).astype(jnp.float32) * scale
        p = jax.nn.softmax(s, axis=-1).astype(v.dtype)
        return jnp.einsum('bhgqk,bkhd->bqhgd', p, v)

    o = lax.map(step, qb)
    return o.transpose(1, 0, 2, 3, 4, 5).reshape(b, sq, hk * g * v.shape[-1])

def _mla_q(h, w_dq, q_norm, w_uq, rows, cols):
    b, s, _ = h.shape
    q = (_rms_norm(h @ w_dq, q_norm) @ w_uq).reshape(b, s, MLA_HEADS, MLA_NOPE + MLA_ROPE)
    q_nope, q_pe = q[..., :MLA_NOPE], q[..., MLA_NOPE:]
    if rows is not None:
        q_pe = _rope_2d(q_pe, rows, cols)
    return jnp.concatenate([q_nope, q_pe], -1)

def _mla_kv(h, w_dkv, kv_norm, w_ukv, rows, cols):
    b, s, _ = h.shape
    ckv = h @ w_dkv
    c_kv, k_pe = ckv[..., :MLA_KV_RANK], ckv[..., MLA_KV_RANK:]
    kv = (_rms_norm(c_kv, kv_norm) @ w_ukv).reshape(b, s, MLA_HEADS, MLA_NOPE + MLA_V)
    k_nope, v = kv[..., :MLA_NOPE], kv[..., MLA_NOPE:]
    k_pe = k_pe[:, :, None, :]
    if rows is not None:
        k_pe = _rope_2d(k_pe, rows, cols)
    k = jnp.concatenate([k_nope, jnp.broadcast_to(k_pe, (b, s, MLA_HEADS, MLA_ROPE))], -1)
    return k, v

def _mla_mixer(h, hc, w_dq, q_norm, w_uq, w_dkv, kv_norm, w_ukv, w_o, need_ctx):
    rows, cols = _grid_positions(h.shape[1])
    scale = (MLA_NOPE + MLA_ROPE) ** -0.5
    q = _mla_q(h, w_dq, q_norm, w_uq, rows, cols)
    k, v = _mla_kv(h, w_dkv, kv_norm, w_ukv, rows, cols)
    kc, vc = _mla_kv(hc, w_dkv, kv_norm, w_ukv, None, None)
    k_all = jnp.concatenate([kc, k], 1)
    v_all = jnp.concatenate([vc, v], 1)
    out = _block_attention(q[:, :, :, None], k_all, v_all, scale) @ w_o
    out_c = None
    if need_ctx:
        qc = _mla_q(hc, w_dq, q_norm, w_uq, None, None)
        out_c = _block_attention(qc[:, :, :, None], kc, vc, scale) @ w_o
    return out, out_c

def _na_mixer(h, hc, w_qkv, b_qkv, rpb, w_o, need_ctx):
    b, s, _ = h.shape
    n_rows = s // GRID_W
    kr = min(NA_WIN_ROWS, n_rows)
    scale = NA_HEAD_DIM ** -0.5

    def proj(t):
        qkv = (t @ w_qkv + b_qkv).reshape(t.shape[0], t.shape[1], 3, NA_HEADS, NA_HEAD_DIM)
        return qkv[:, :, 0], qkv[:, :, 1], qkv[:, :, 2]

    q, k, v = proj(h)
    qc, kc, vc = proj(hc)
    grid = (b, n_rows, GRID_W, NA_HEADS, NA_HEAD_DIM)
    q_grid, k_grid, v_grid = q.reshape(grid), k.reshape(grid), v.reshape(grid)

    r_idx = jnp.arange(n_rows, dtype=jnp.int32)
    row_start = jnp.clip(r_idx - kr // 2, 0, n_rows - kr)
    c_idx = jnp.arange(GRID_W, dtype=jnp.int32)
    col_start = jnp.clip(c_idx - NA_WIN_COLS // 2, 0, GRID_W - NA_WIN_COLS)
    col_valid = (c_idx[None, :] >= col_start[:, None]) & (c_idx[None, :] < col_start[:, None] + NA_WIN_COLS)
    mask = jnp.tile(col_valid, (1, kr))
    dc = jnp.clip(c_idx[None, :] - c_idx[:, None] + NA_WIN_COLS - 1, 0, 2 * NA_WIN_COLS - 2)
    rpb_cols = rpb[:, :, dc]

    def row_step(args):
        r, rs = args
        q_row = lax.dynamic_index_in_dim(q_grid, r, axis=1, keepdims=False)
        k_strip = lax.dynamic_slice_in_dim(k_grid, rs, kr, axis=1).reshape(b, kr * GRID_W, NA_HEADS, NA_HEAD_DIM)
        v_strip = lax.dynamic_slice_in_dim(v_grid, rs, kr, axis=1).reshape(b, kr * GRID_W, NA_HEADS, NA_HEAD_DIM)
        dr = rs + jnp.arange(kr, dtype=jnp.int32) - r + NA_WIN_ROWS - 1
        bias = jnp.take(rpb_cols, dr, axis=1).transpose(0, 2, 1, 3).reshape(NA_HEADS, GRID_W, kr * GRID_W)
        s_lat = jnp.einsum('bqhd,bkhd->bhqk', q_row, k_strip).astype(jnp.float32) * scale + bias
        s_lat = jnp.where(mask, s_lat, -jnp.inf)
        s_ctx = jnp.einsum('bqhd,bkhd->bhqk', q_row, kc).astype(jnp.float32) * scale
        p = jax.nn.softmax(jnp.concatenate([s_ctx, s_lat], -1), axis=-1).astype(v.dtype)
        return jnp.einsum('bhqk,bkhd->bqhd', p, jnp.concatenate([vc, v_strip], 1))

    o = lax.map(row_step, (r_idx, row_start))
    out = o.transpose(1, 0, 2, 3, 4).reshape(b, s, NA_HEADS * NA_HEAD_DIM) @ w_o
    out_c = None
    if need_ctx:
        out_c = _block_attention(qc[:, :, :, None], kc, vc, scale) @ w_o
    return out, out_c

def _gqa_proj(t, w_qkv, q_norm, k_norm, rows, cols):
    bb, ss, _ = t.shape
    nq = GQA_Q_HEADS * GQA_HEAD_DIM
    nk = GQA_KV_HEADS * GQA_HEAD_DIM
    qkv = t @ w_qkv
    q = _rms_norm(qkv[..., :nq].reshape(bb, ss, GQA_Q_HEADS, GQA_HEAD_DIM), q_norm)
    k = _rms_norm(qkv[..., nq:nq + nk].reshape(bb, ss, GQA_KV_HEADS, GQA_HEAD_DIM), k_norm)
    v = qkv[..., nq + nk:].reshape(bb, ss, GQA_KV_HEADS, GQA_HEAD_DIM)
    if rows is not None:
        q = _rope_2d(q, rows, cols)
        k = _rope_2d(k, rows, cols)
    return q.reshape(bb, ss, GQA_KV_HEADS, GQA_GROUP, GQA_HEAD_DIM), k, v

def _gqa_mixer(h, hc, w_qkv, q_norm, k_norm, w_o, need_ctx):
    rows, cols = _grid_positions(h.shape[1])
    scale = GQA_HEAD_DIM ** -0.5
    q, k, v = _gqa_proj(h, w_qkv, q_norm, k_norm, rows, cols)
    qc, kc, vc = _gqa_proj(hc, w_qkv, q_norm, k_norm, None, None)
    out = _block_attention(q, jnp.concatenate([kc, k], 1), jnp.concatenate([vc, v], 1), scale) @ w_o
    out_c = None
    if need_ctx:
        out_c = _block_attention(qc, kc, vc, scale) @ w_o
    return out, out_c

def _mlp(h, w1, w2):
    return jnp.square(jax.nn.relu(h @ w1)) @ w2

def second_inputs(seed: int = 0) -> dict:
    key = jax.random.key(seed)
    ks = iter(jax.random.split(key, 32))
    beta = (8.0 * DEPTH_2) ** -0.25
    n_a = len(range(0, DEPTH_2, N_MIXERS))
    n_b = len(range(1, DEPTH_2, N_MIXERS))
    n_c = len(range(2, DEPTH_2, N_MIXERS))
    D = D_MODEL

    def nrm(shape, s=1.0):
        return jax.random.normal(next(ks), shape, jnp.float32) * s

    def w(shape, fan_in, g=1.0):
        return nrm(shape, g * fan_in ** -0.5)

    def gain(shape):
        return 1.0 + nrm(shape, 0.05)

    return {
        "x": nrm((BATCH, SEQ, D)),
        "c": nrm((BATCH, D)),
        "ctx": nrm((BATCH, CTX_LEN, D)),
        "c_ctx": nrm((D,)),
        "ada_w": w((DEPTH_2, D, 6 * D), D),
        "ada_b": nrm((DEPTH_2, 6 * D), 0.02),
        "ln1_g": gain((DEPTH_2, D)),
        "ln1_b": nrm((DEPTH_2, D), 0.02),
        "ln2_g": gain((DEPTH_2, D)),
        "ln2_b": nrm((DEPTH_2, D), 0.02),
        "mlp_w1": w((DEPTH_2, D, D_FF_2), D),
        "mlp_w2": w((DEPTH_2, D_FF_2, D), D_FF_2, beta),
        "mla_w_dq": w((n_a, D, MLA_Q_RANK), D),
        "mla_q_norm": gain((n_a, MLA_Q_RANK)),
        "mla_w_uq": w((n_a, MLA_Q_RANK, MLA_HEADS * (MLA_NOPE + MLA_ROPE)), MLA_Q_RANK),
        "mla_w_dkv": w((n_a, D, MLA_KV_RANK + MLA_ROPE), D),
        "mla_kv_norm": gain((n_a, MLA_KV_RANK)),
        "mla_w_ukv": w((n_a, MLA_KV_RANK, MLA_HEADS * (MLA_NOPE + MLA_V)), MLA_KV_RANK),
        "mla_w_o": w((n_a, MLA_HEADS * MLA_V, D), MLA_HEADS * MLA_V, beta),
        "na_w_qkv": w((n_b, D, 3 * NA_HEADS * NA_HEAD_DIM), D),
        "na_b_qkv": nrm((n_b, 3 * NA_HEADS * NA_HEAD_DIM), 0.02),
        "na_rpb": nrm((n_b, NA_HEADS, 2 * NA_WIN_ROWS - 1, 2 * NA_WIN_COLS - 1), 0.1),
        "na_w_o": w((n_b, NA_HEADS * NA_HEAD_DIM, D), NA_HEADS * NA_HEAD_DIM, beta),
        "gqa_w_qkv": w((n_c, D, (GQA_Q_HEADS + 2 * GQA_KV_HEADS) * GQA_HEAD_DIM), D),
        "gqa_q_norm": gain((n_c, GQA_HEAD_DIM)),
        "gqa_k_norm": gain((n_c, GQA_HEAD_DIM)),
        "gqa_w_o": w((n_c, GQA_Q_HEADS * GQA_HEAD_DIM, D), GQA_Q_HEADS * GQA_HEAD_DIM, beta),
    }

def second_block(x, c, ctx, c_ctx, ada_w, ada_b, ln1_g, ln1_b, ln2_g, ln2_b, mlp_w1, mlp_w2,
              mla_w_dq, mla_q_norm, mla_w_uq, mla_w_dkv, mla_kv_norm, mla_w_ukv, mla_w_o,
              na_w_qkv, na_b_qkv, na_rpb, na_w_o,
              gqa_w_qkv, gqa_q_norm, gqa_k_norm, gqa_w_o):
    alpha = (2.0 * DEPTH_2) ** 0.25
    for i in range(DEPTH_2):
        kind, j = i % N_MIXERS, i // N_MIXERS
        need_ctx = i < DEPTH_2 - 1
        mod = (jax.nn.silu(c) @ ada_w[i] + ada_b[i])[:, None, :]
        mod_c = jax.nn.silu(c_ctx) @ ada_w[i] + ada_b[i]
        sh1, sc1, g1, sh2, sc2, g2 = jnp.split(mod, 6, axis=-1)
        csh1, csc1, cg1, csh2, csc2, cg2 = jnp.split(mod_c, 6, axis=-1)

        h = x * (1 + sc1) + sh1
        hc = ctx * (1 + csc1) + csh1
        if kind == 0:
            y, yc = _mla_mixer(h, hc, mla_w_dq[j], mla_q_norm[j], mla_w_uq[j], mla_w_dkv[j],
                               mla_kv_norm[j], mla_w_ukv[j], mla_w_o[j], need_ctx)
        elif kind == 1:
            y, yc = _na_mixer(h, hc, na_w_qkv[j], na_b_qkv[j], na_rpb[j], na_w_o[j], need_ctx)
        else:
            y, yc = _gqa_mixer(h, hc, gqa_w_qkv[j], gqa_q_norm[j], gqa_k_norm[j], gqa_w_o[j], need_ctx)
        x = _layer_norm(alpha * x + g1 * y, ln1_g[i], ln1_b[i])
        if need_ctx:
            ctx = _layer_norm(alpha * ctx + cg1 * yc, ln1_g[i], ln1_b[i])

        x = _layer_norm(alpha * x + g2 * _mlp(x * (1 + sc2) + sh2, mlp_w1[i], mlp_w2[i]), ln2_g[i], ln2_b[i])
        if need_ctx:
            ctx = _layer_norm(alpha * ctx + cg2 * _mlp(ctx * (1 + csc2) + csh2, mlp_w1[i], mlp_w2[i]),
                              ln2_g[i], ln2_b[i])
    return x


def setup_inputs(seed=0):
    out = dict(first_inputs(seed))
    for name, value in second_inputs(seed + 1).items():
        if name != "x":
            out[name + "_2"] = value
    return out


def reference(
    x, norm_mix, norm_ffn, norm_final, ffn_w_gate, ffn_w_up, ffn_w_down, nsa_w_in, nsa_w_out,
    nsa_cmp_pos_k, nsa_cmp_pos_v, nsa_cmp_k_w1, nsa_cmp_k_w2, nsa_cmp_v_w1, nsa_cmp_v_w2,
    moba_w_in, moba_w_out, conv_w_in, conv_w, conv_w_out, c_2, ctx_2, c_ctx_2, ada_w_2, ada_b_2,
    ln1_g_2, ln1_b_2, ln2_g_2, ln2_b_2, mlp_w1_2, mlp_w2_2, mla_w_dq_2, mla_q_norm_2,
    mla_w_uq_2, mla_w_dkv_2, mla_kv_norm_2, mla_w_ukv_2, mla_w_o_2, na_w_qkv_2, na_b_qkv_2,
    na_rpb_2, na_w_o_2, gqa_w_qkv_2, gqa_q_norm_2, gqa_k_norm_2, gqa_w_o_2,
):
    x = first_block(
        x, norm_mix, norm_ffn, norm_final, ffn_w_gate, ffn_w_up, ffn_w_down, nsa_w_in,
        nsa_w_out, nsa_cmp_pos_k, nsa_cmp_pos_v, nsa_cmp_k_w1, nsa_cmp_k_w2, nsa_cmp_v_w1,
        nsa_cmp_v_w2, moba_w_in, moba_w_out, conv_w_in, conv_w, conv_w_out,
    )
    return second_block(
        x, c_2, ctx_2, c_ctx_2, ada_w_2, ada_b_2, ln1_g_2, ln1_b_2, ln2_g_2, ln2_b_2, mlp_w1_2,
        mlp_w2_2, mla_w_dq_2, mla_q_norm_2, mla_w_uq_2, mla_w_dkv_2, mla_kv_norm_2, mla_w_ukv_2,
        mla_w_o_2, na_w_qkv_2, na_b_qkv_2, na_rpb_2, na_w_o_2, gqa_w_qkv_2, gqa_q_norm_2,
        gqa_k_norm_2, gqa_w_o_2,
    )


_drawn_inputs = setup_inputs


def setup_inputs(seed=0):
    import zlib

    import numpy as np

    out = dict(_drawn_inputs(seed))
    spreads = {}
    factors = {'norm_final': 3.011,
     'nsa_cmp_pos_k': 6.396,
     'mla_q_norm_2': 8.0,
     'mla_kv_norm_2': 8.0,
     'na_b_qkv_2': 8.0,
     'na_rpb_2': 8.0}
    for name, (base, spread) in spreads.items():
        noise = np.random.default_rng([zlib.crc32(name.encode()), seed]).standard_normal(out[name].shape)
        drawn = base * np.exp(spread * noise) if base else spread * noise
        out[name] = __import__('jax').numpy.asarray(drawn.astype(out[name].dtype))
    for name, factor in factors.items():
        out[name] = (out[name] * factor).astype(out[name].dtype)
    return out
```

```python
from contextlib import ExitStack, contextmanager

import concourse.bass as bass
from concourse import mybir
from concourse.alu_op_type import AluOpType as ALU
import numpy as np

ACT = mybir.ActivationFunctionType
F32 = mybir.dt.float32
F32R = mybir.dt.float32r
AX_X = mybir.AxisListType.X

P = 128
D = 1024
S = 256
KD = D // P
HD = 64
GROUPS, REP, HEADS = 4, 4, 16
KV = GROUPS * HD
CMP_BLOCK, CMP_STRIDE, CMP_HIDDEN = 32, 16, 256
N_CMP = (S - CMP_BLOCK) // CMP_STRIDE + 1
CS = 16
D_FF = -(-8 * D // (3 * 256)) * 256
FT = D_FF // P
D_FF_2 = 4 * D
MLA_H, NOPE, ROPE, MLA_V, Q_RANK, KV_RANK = 8, 128, 64, 128, 512, 256
QR, KR = Q_RANK // P, KV_RANK // P
GRID_W = 64
NA_ROWS, NA_COLS = 8, 16
ROPE_THETA = 10000.0
RMS_EPS, LN_EPS = 1e-6, 1e-5
ALPHA = float(np.float32((2.0 * 2) ** 0.25))
NEG = -1e30
ADA_CHUNKS = 6
MOD_TILES = 2 * ADA_CHUNKS * KD

LAT = slice(S, 2 * S)
CTX = slice(0, S)
ALL = slice(0, 2 * S)

TILES = 16
UC = TILES * P
HALF_FT = FT // 2
SMALL_UNIT = 2 * P + 2 * HD + KD * 3 * HEADS
ADA_PER_LAYER = 12

PROGRAM = [("nsa", 0), ("ffn", 0), ("moba", 0), ("ffn", 1), ("conv", 0), ("ffn", 2), ("nsa", 1), ("ffn", 3),
           ("enter", 0), ("mla", 0), ("mlp", 0), ("na", 0), ("mlp", 1)]
WIDTHS = {
    "nsa": [UC] * 14 + [SMALL_UNIT] + [UC] * 6,
    "moba": [UC] * 18,
    "conv": [UC] * 18,
    "ffn": [UC] * 32 + [HALF_FT * P] * 16,
    "enter": [],
    "mla": [UC] * 14,
    "na": [UC] * 16,
    "mlp": [UC] * 32,
}
UNIT_WIDTHS = [w for stage, _ in PROGRAM for w in WIDTHS[stage]]
U = len(UNIT_WIDTHS)

SMALL = {}
_at = 0
for _name, _width in [
    ("norm_mix", 4 * KD), ("norm_ffn", 4 * KD), ("norm_final", KD), ("c", 2 * KD), ("ada_b", MOD_TILES),
    ("ln1_g", 2 * KD), ("ln1_b", 2 * KD), ("ln2_g", 2 * KD), ("ln2_b", 2 * KD), ("q_norm", QR), ("kv_norm", KR),
    ("na_bq", KD), ("na_bk", KD), ("conv_w", 3 * KD), ("pos", 2 * 2 * CMP_BLOCK // 2), ("rms_eps", 1), ("ln_eps", 1),
    ("zero", 1), ("valid", 2), ("cmp_mask", 2 * CS), ("causal", 2 * P), ("ident", P), ("ones", P),
    ("cos", S), ("sin", S),
]:
    SMALL[_name] = slice(_at, _at + _width)
    _at += _width
N_SMALL = _at


class Num:

    def __init__(self, c, stride=0, reg=None):
        self.c, self.stride, self.reg = c, stride, reg

    def __add__(self, n):
        return Num(self.c + n, self.stride, self.reg)

    def __sub__(self, n):
        return self + -n

    @property
    def v(self):
        return self.c if self.reg is None else self.reg * self.stride + self.c

    @property
    def odd(self):
        return self.c % 2

    @property
    def half(self):
        return Num(self.c // 2, self.stride // 2, self.reg)

    def times(self, n):
        return Num(self.c * n, self.stride * n, self.reg)


class Counts:

    def __init__(self):
        self.n = {"unit": 0, "A": 0, "D": 0, "M": 0, "mid": 0, "hid": 0, "relu": 2, "res": 0}
        self.reg, self.per = None, {}

    def next(self, name):
        self.n[name] += 1
        return Num(self.n[name] - 1, self.per.get(name, 0), self.reg)

    def peek(self, name):
        return Num(self.n[name], self.per.get(name, 0), self.reg)

    @contextmanager
    def loop(self, eng, times, **per):
        before = dict(self.n)
        with eng.Fori(0, times) as i:
            self.reg, self.per = i, per
            yield i
            assert self.n == {k: v + per.get(k, 0) for k, v in before.items()}, (before, self.n, per)
        self.reg, self.per = None, {}
        self.n = {k: v + times * per.get(k, 0) for k, v in before.items()}


def halves(width):
    cut = -(-width // (2 * P)) * P
    return slice(0, cut), slice(cut, width)


def program(nc, weights, small, x_t, ctx_t, na_bias, na_bv, out_t):
    with ExitStack() as ctx:
        def sem(name):
            return ctx.enter_context(nc.semaphore(name))

        def sb(name, shape, dt=F32):
            return ctx.enter_context(nc.sbuf_tensor(name, shape, dt))

        stage = sb("stage", [P, 2, UC])
        w_hi = sb("w_hi", [P, 2, UC], F32R)
        w_lo = sb("w_lo", [P, 2, UC], F32R)
        X = sb("X", [P, KD, 2 * S])
        a_hi = sb("a_hi", [P, KD, 2 * S], F32R)
        a_lo = sb("a_lo", [P, KD, 2 * S], F32R)
        hid_hi = sb("hid_hi", [P, FT * S], F32R)
        hid_lo = sb("hid_lo", [P, FT * S], F32R)
        qk = sb("qk", [P, 2 * KD, 2 * S])
        v_sb = sb("v_sb", [P, 4, D])
        pe_sb = sb("pe_sb", [P, 5, 2 * S])
        p_ring = sb("p_ring", [P, 3, 2 * S])
        t_ring = sb("t_ring", [P, 2, 2 * S])
        sm = sb("sm", [P, N_SMALL])
        mod_raw = sb("mod_raw", [P, MOD_TILES, 4])
        mod = sb("mod", [P, MOD_TILES, 2])
        c_parts = sb("c_parts", [P, KD, 4], F32R)
        c_act = sb("c_act", [P, KD, 2])
        gate = sb("gate", [P, 2, 3 * HEADS])
        k_cmp = sb("k_cmp", [P, GROUPS, CS])
        negmax = sb("negmax", [P, 4, 2])
        sums = sb("sums", [P, 4, 2])
        recip = sb("recip", [P, 4, 2])
        cmp_max = sb("cmp_max", [P, 2 * HEADS])
        cmp_sum = sb("cmp_sum", [P, 2 * HEADS])

        q_sb, k_sb = qk[:, 0:KD], qk[:, KD:2 * KD]
        rstd = p_ring[:, 2, :]
        sq_sum = p_ring[:, 0, 0:S]
        y_acc = q_sb

        ps = ctx.enter_context(nc.psum_tensor("ps", [P, 8, 512], F32))
        BANK = {"A": 0, "D": 2, "M": 5}
        STAT, S0, T0, O0 = 7, 0, 3, 5
        CMP_BANK = (7, 4)

        def col(name, i=0, n=1):
            return sm[:, SMALL[name].start + i:SMALL[name].start + i + n]

        ident, ones = col("ident", 0, P), col("ones", 0, P)

        small_loaded, x_loaded = sem("small_loaded"), sem("x_loaded")
        landed = [sem("landed0"), sem("landed1")]
        hi_split, lo_split = sem("hi_split"), sem("lo_split")
        unit_done = sem("unit_done")
        mid_ready = sem("mid_ready")
        taken = {r: sem(f"taken_{r}") for r in "ADM"}
        c_ready, c_hi = sem("c_ready"), sem("c_hi")
        sq_ready, sq_used = sem("sq_ready"), sem("sq_used")
        res_sq, res_acc, sum_done = sem("res_sq"), sem("res_acc"), sem("sum_done")
        std_ready, mean_ready, mean_sum = sem("std_ready"), sem("mean_ready"), sem("mean_sum")
        centered, x_mixed, x_norm = sem("centered"), sem("x_mixed"), sem("x_norm")
        normed, norm_hi, operand = sem("normed"), sem("norm_hi"), sem("operand")
        hid_f, hid_h, hid_ready = sem("hid_f"), sem("hid_h"), sem("hid_ready")
        dve_step, act_step = sem("dve_step"), sem("act_step")
        att = {n: {e: sem(f"{n}_{e}") for e in ("s_ready", "s_taken", "exp_done", "p_ready", "t_ready",
                                                "t_taken", "pv_done", "o_hi", "o_ready")}
               for n in ("nsa0", "nsa1", "moba0", "mla0", "na0")}
        nsa = [{e: sem(f"{e}{j}") for e in ("shifted", "blocks", "blocks_hi", "blocks_ready", "gelu", "gelu_ready", "cmp_scores",
                                            "cmp_shifted", "cmp_exp", "cmp_p", "cmp_t", "cmp_t_taken")}
               for j in range(2)]
        conv_z_ready, conv_hi, conv_ready = sem("conv_z_ready"), sem("conv_hi"), sem("conv_ready")
        ctx_loaded, rope_ready = sem("ctx_loaded"), sem("rope_ready")
        bias_loaded = [sem(f"bias_loaded{i}") for i in range(4)]
        bv_loaded, stored, x_final = sem("bv_loaded"), sem("stored"), sem("x_final")

        def wait(eng, s, n):
            if isinstance(n, Num):
                if n.reg is not None:
                    assert n.c > 0
                    eng.wait_ge(s, n.v)
                    return
                n = n.c
            if n > 0:
                eng.wait_ge(s, n)

        def unit(cnt, rings):
            u, made = cnt.next("unit"), []
            for j, ring in enumerate(rings):
                p = cnt.next(ring)
                last = j == len(rings) - 1
                made.append((BANK[ring] + p.odd, p,
                             (unit_done, u + 1) if last else (mid_ready, cnt.next("mid") + 1)))
            return u, made

        def causal_item(tile, q_rows, q, k_tile, v_of, out_rows, first, last, r_of=None, cmp=None):
            kk = k_sb[q_rows, k_tile, 0:S]
            return dict(
                tile=tile, last=last, cols=3 * P, gate=r_of,
                scores=[(slice(0, P), [(q[:, 0:P], kk[:, 0:P])]), (slice(P, 3 * P), [(q[:, P:S], kk)])],
                rows=[(slice(0, P), col("causal", P, P)), (slice(P, 3 * P), col("causal", 0, 2 * P))],
                turns=[(0, 0), (P, P), (2 * P, 2 * P)],
                pv=([(cmp[0], cmp[1], slice(0, S), out_rows)] if cmp else [])
                + [(v_of(0), slice(0, S), slice(0, S), out_rows), (v_of(1), slice(S, S + P), slice(P, S), out_rows)],
                first=first)

        def half(e):
            return slice(HD * e, HD * e + HD)

        def nsa_items():
            items = []
            for pair in range(2):
                for r in range(REP):
                    for e in range(2):
                        g = 2 * pair + e
                        h = g * REP + r
                        for br in range(2):
                            cmp = None
                            if br == 0:
                                cmp = (v_sb[:, 3, (g * REP + r) * HD:(g * REP + r + 1) * HD],
                                       v_sb[:, 2, g * S:(g + 1) * S])
                            items.append(causal_item(
                                pair * REP + r, half(e), q_sb[half(e), pair * REP + r, 0:S], 2 * br + pair,
                                lambda kt, br=br, g=g: v_sb[:, kt, br * KV + g * HD:br * KV + (g + 1) * HD],
                                half(e), br == 0, e == 1 and br == 1, (1 + br) * HEADS + h, cmp))
            return items

        def moba_items():
            return [causal_item(h // 2, half(h % 2), q_sb[half(h % 2), h // 2, 0:S], h // 2,
                                lambda kt, h=h: v_sb[:, kt, h * HD:(h + 1) * HD], half(h % 2), True, h % 2 == 1)
                    for h in range(HEADS)]

        def mla_items():
            items = []
            for h in range(MLA_H):
                rows, pt = half(h % 2), h // 2

                def score(qs, ks, h=h, rows=rows, pt=pt):
                    return [(q_sb[:, h, qs], k_sb[:, h, ks]), (pe_sb[rows, pt, qs], pe_sb[rows, 4, ks])]

                def v_of(kt, h=h):
                    return v_sb[:, kt, h * MLA_V:(h + 1) * MLA_V]

                full = slice(0, P)
                none = col("zero")
                items.append(dict(
                    tile=h, last=False, first=True, cols=4 * P, gate=None,
                    scores=[(slice(S * j, S * j + S), score(slice(P * j, P * j + P), CTX)) for j in range(2)],
                    rows=[(slice(S * j, S * j + S), none.to_broadcast([P, S])) for j in range(2)],
                    turns=[(0, 0), (P, 2 * P), (2 * P, P), (3 * P, 3 * P)],
                    pv=[(v_of(kt), slice(S * kt, S * kt + S), CTX, full) for kt in range(2)]))
                for j in range(2):
                    qs = slice(S + P * j, S + P * j + P)
                    items.append(dict(
                        tile=h, last=j == 1, first=True, cols=4 * P, gate=None,
                        scores=[(ALL, score(qs, ALL))], rows=[(ALL, none.to_broadcast([P, 2 * S]))],
                        turns=[(P * i, P * i) for i in range(4)],
                        pv=[(v_of(kt), slice(P * kt, P * kt + P), qs, full) for kt in range(4)]))
            return items

        bias_ring = pe_sb

        def na_items():
            items = []
            for h in range(HEADS):
                for j in range(2):
                    rows, i = half(h % 2), 2 * h + j
                    qs = slice(S + P * j, S + P * j + P)
                    items.append(dict(
                        tile=h // 2, last=h % 2 == 1 and j == 1, first=True, cols=4 * P, gate=None, bias=(h, j),
                        scores=[(ALL, [(q_sb[rows, h // 2, qs], k_sb[rows, h // 2, ALL])])],
                        rows=[(ALL, bias_ring[:, i % 4, :])],
                        turns=[(P * n, P * n) for n in range(4)],
                        pv=[(v_sb[:, kt, h * HD:(h + 1) * HD], slice(P * kt, P * kt + P), slice(P * j, P * j + P), rows)
                            for kt in range(4)]))
            return items

        ITEMS = {"nsa0": nsa_items(), "nsa1": nsa_items(), "moba0": moba_items(), "mla0": mla_items(), "na0": na_items()}
        NEG_SCALE = {"nsa0": -HD ** -0.5, "nsa1": -HD ** -0.5, "moba0": -HD ** -0.5,
                     "mla0": -float(np.float32((NOPE + ROPE) ** -0.5)), "na0": -1.0}
        OUT_COLS = {"nsa0": S, "nsa1": S, "moba0": S, "mla0": 2 * S, "na0": S}
        OUT_TOK = {"nsa0": LAT, "nsa1": LAT, "moba0": LAT, "mla0": ALL, "na0": LAT}

        blk_f = v_sb[:, 2:4, :].rearrange("p a n -> p (a n)")
        NB = 2 * 16 * GROUPS * CS
        blk_hi, blk_lo = hid_hi[:, 0:NB], hid_lo[:, 0:NB]
        kg_hi = hid_hi[:, NB:NB + 2 * GROUPS * CS]
        kg_lo = hid_lo[:, NB:NB + 2 * GROUPS * CS]
        G0 = NB + 2 * GROUPS * CS
        GN = 2 * GROUPS * REP * 32
        vg_hi, vg_lo = hid_hi[:, G0:G0 + GN], hid_lo[:, G0:G0 + GN]
        cmp_s = pe_sb[:, 0, :]
        gel = pe_sb[:, 1, 0:4 * GROUPS * CS]
        p_cmp = k_sb[:, 6:8, :].rearrange("p a n -> p (a n)")
        cq_hi, cq_lo = (h[:, 0:QR * 2 * S].rearrange("p (k t) -> p k t", k=QR) for h in (hid_hi, hid_lo))
        ckv_hi, ckv_lo = (h[:, QR * 2 * S:(QR + KR) * 2 * S].rearrange("p (k t) -> p k t", k=KR) for h in (hid_hi, hid_lo))
        cq_raw = v_sb[:, 0:2, :].rearrange("p a (b t) -> p (a b) t", b=2)
        ckv_raw = v_sb[:, 2, :].rearrange("p (b t) -> p b t", b=2)
        mlp_hi, mlp_lo = (h[:, 0:KD * 2 * S].rearrange("p (k t) -> p k t", k=KD) for h in (hid_hi, hid_lo))
        by_hi, by_lo = (h[:, 0:KD * S].rearrange("p (k t) -> p k t", k=KD) for h in (hid_hi, hid_lo))
        conv_z = v_sb[:, 0:2, :].rearrange("p a (b t) -> p (a b) t", b=4)

        def mods(layer, chunk, k, s):
            j = (layer * ADA_CHUNKS + chunk) * KD + k
            return mod[:, j, s:s + 1]

        block = ctx.enter_context(nc.Block())

        @block.sync
        def _(sp):
            def load(u, width, odd, first):
                if not first:
                    wait(sp, lo_split, (u - 1).times(2))
                sp.dma_start(stage[:, odd, 0:width], weights[:, bass.ds(u.times(UC).v, width)]).then_inc(landed[odd], 16)

            u = 0
            while u < U:
                width, n = UNIT_WIDTHS[u], 1
                while u + n < U and UNIT_WIDTHS[u + n] == width:
                    n += 1
                if u == 0:
                    load(Num(0), width, 0, True)
                    sp.dma_start(X[:, :, CTX], ctx_t.rearrange("(k p) t -> p k t", p=P)).then_inc(ctx_loaded, 16)
                    load(Num(1), width, 1, True)
                    u, n = 2, n - 2
                if n >= 4:
                    with sp.Fori(0, n // 2) as i:
                        for r in range(2):
                            load(Num(u + r, 2, i), width, (u + r) % 2, False)
                    u, n = u + n // 2 * 2, n % 2
                for r in range(n):
                    load(Num(u + r), width, (u + r) % 2, False)
                u += n
            sp.wait_ge(x_final, KD)
            sp.dma_start(out_t.rearrange("(k p) t -> p k t", p=P), X[:, :, LAT]).then_inc(stored, 16)
            sp.wait_ge(stored, 16)

        @block.tensor
        def _(pe):
            cnt = Counts()
            n = dict(sq=0, tile=0, hid=0, mean=0, res=0, unit=None, fresh=None)

            def mm(out, stationary, moving, start, stop):
                return nc.tensor.matmul(out, stationary, moving, start=start, stop=stop)

            def begin(u):
                wait(pe, lo_split, u.times(2) + 1)
                n["unit"] = u

            def weights_at(c):
                u = n["unit"]
                if u is not None and c.stop > halves(UNIT_WIDTHS[u.c])[0].stop:
                    wait(pe, lo_split, u.times(2) + 2)
                    n["unit"] = None

            def fm(out, slot, tile, xs, start=True, stop=True, width=P):
                for k, (xh, xl) in enumerate(xs):
                    c = slice((tile + k) * width, (tile + k + 1) * width)
                    weights_at(c)
                    operand_at(k)
                    mm(out, w_hi[:, slot, c], xh, start and k == 0, False)
                    mm(out, w_hi[:, slot, c], xl, False, False)
                    last = mm(out, w_lo[:, slot, c], xh, False, stop and k == len(xs) - 1)
                return last

            def tm(out, slot, cols, xs):
                for k, (xh, xl) in enumerate(xs):
                    c = cols(k)
                    weights_at(c)
                    mm(out, xh, w_hi[:, slot, c], k == 0, False)
                    mm(out, xl, w_hi[:, slot, c], False, False)
                    last = mm(out, xh, w_lo[:, slot, c], False, k == len(xs) - 1)
                return last

            def start_unit(rings):
                u, made = unit(cnt, rings)
                begin(u)
                return u, made

            def start_product(ring, p):
                wait(pe, taken[ring], p - 1)

            def fm_unit(rings, xs, tiles=None):
                u, made = start_unit(rings)
                T = xs[0][0].shape[-1]
                for j, (bank, p, (ready, _)) in enumerate(made):
                    start_product(rings[j], p)
                    fm(ps[:, bank, 0:T], u.odd, j * len(xs), xs).then_inc(ready, 1)

            def tm_unit(xs_of, halves, width, ncols):
                u, made = start_unit("D" * len(halves))
                for (bank, p, (ready, _)), (tt, c0) in zip(made, halves):
                    start_product("D", p)
                    tm(ps[:, bank, 0:ncols], u.odd, lambda k: slice(k * width + c0, k * width + c0 + ncols),
                       xs_of(tt)).then_inc(ready, 1)

            def ada_unit():
                u, [(bank, p, (ready, _))] = start_unit("M")
                start_product("M", p)
                for m in range(2):
                    out = ps[:, bank, 4 * m:4 * m + 4]
                    for k in range(KD):
                        c = slice((m * KD + k) * P, (m * KD + k + 1) * P)
                        weights_at(c)
                        mm(out, w_hi[:, u.odd, c], c_parts[:, k, :], k == 0, False)
                        last = mm(out[:, 0:2], w_lo[:, u.odd, c], c_parts[:, k, 0:2], False, k == KD - 1)
                last.then_inc(ready, 1)

            def parts(hi, lo, cols=LAT):
                return [(hi[:, k, cols], lo[:, k, cols]) for k in range(hi.shape[1])]

            def sum_squares(nk, T):
                for k in range(nk):
                    pe.wait_ge(sq_ready, n["sq"] + k + 1)
                    mm(ps[:, STAT, 0:T], ones, t_ring[:, (n["sq"] + k) % 2, 0:T], k == 0, k == nk - 1).then_inc(sq_used, 1)
                n["sq"] += nk

            def sum_residual():
                n["res"] += KD
                pe.wait_ge(res_acc, n["res"])
                mm(ps[:, STAT, 0:S], ones, sq_sum, True, True).then_inc(sum_done, 1)

            def operands(nk=KD):
                n["fresh"] = n["tile"]
                n["tile"] += nk

            def operand_at(k):
                if n["fresh"] is not None:
                    pe.wait_ge(operand, n["fresh"] + k + 1)
                    if n["fresh"] + k + 1 == n["tile"]:
                        n["fresh"] = None

            def drained():
                for r in "AD":
                    wait(pe, taken[r], cnt.peek(r))

            def out_units(src):
                for _ in range(4):
                    fm_unit("DD", src)

            def attention(name, before_turns=None):
                a, items = att[name], ITEMS[name]
                pv_of = []
                for i in range(len(items) + 3):
                    if i < len(items):
                        it = items[i]
                        if i >= 3:
                            pe.wait_ge(a["s_taken"], i - 2)
                        for c, terms in it["scores"]:
                            for t, (q, k) in enumerate(terms):
                                last = mm(ps[:, S0 + i % 3, c], q, k, t == 0, t == len(terms) - 1)
                        last.then_inc(a["s_ready"], 1)
                    if i == 2 and before_turns:
                        before_turns()
                    if 0 <= i - 2 < len(items):
                        b = i - 2
                        pe.wait_ge(a["p_ready"], b + 1)
                        if b >= 2:
                            pe.wait_ge(a["t_taken"], b - 1)
                        for to, frm in items[b]["turns"]:
                            last = nc.tensor.transpose(ps[:, T0 + b % 2, to:to + P], p_ring[:, b % 3, frm:frm + P], ident)
                        last.then_inc(a["t_ready"], 1)
                    if 0 <= i - 3 < len(items):
                        b = i - 3
                        it = items[b]
                        o = O0 + it["tile"] % 2
                        pe.wait_ge(a["t_taken"], b + 1)
                        if it["tile"] >= 2:
                            pe.wait_ge(a["o_ready"], it["tile"] - 1)
                        for j, (v, t, q, rows) in enumerate(it["pv"]):
                            moving = t_ring[:, b % 2, t] if isinstance(t, slice) else t
                            last = nc.tensor.matmul(ps[rows, o, q], v, moving, start=it["first"] and j == 0,
                                                    stop=j == len(it["pv"]) - 1, skip_group_check=True)
                        last.then_inc(a["pv_done"], 1)

            def out_operands(name):
                pe.wait_ge(att[name]["o_ready"], KD)

            def mixer_ends():
                ada_unit()
                sum_residual()
                ada_unit()

            def run_nsa(j):
                if cnt.n["unit"] == 0:
                    sum_squares(KD, S)
                operands()
                a = parts(a_hi, a_lo)
                for _ in range(2):
                    fm_unit("AA", a)
                for _ in range(4):
                    fm_unit("AA", a)
                for _ in range(2):
                    fm_unit("AA", a)
                for _ in range(2):
                    tm_unit(lambda tt: [(a_hi[:, k, S + tt * P:S + tt * P + P], a_lo[:, k, S + tt * P:S + tt * P + P])
                                        for k in range(KD)], [(0, 0), (1, 0)], KV, KV)
                pe.wait_ge(nsa[j]["blocks_ready"], 1)
                for kv in range(2):
                    for m in range(2):
                        u, [(bank, p, (ready, _))] = start_unit("A")
                        start_product("A", p)
                        N = GROUPS * CS
                        xs = [(blk_hi[:, (kv * 16 + l) * N:(kv * 16 + l + 1) * N], blk_lo[:, (kv * 16 + l) * N:(kv * 16 + l + 1) * N])
                              for l in range(16)]
                        fm(ps[:, bank, 0:N], u.odd, 0, xs).then_inc(ready, 1)
                u, [(gb, gp, (g_ready, _)), (kb, kp, (k_ready, _)), (vb, vp, (v_ready, _))] = start_unit("AAD")
                start_product("A", gp)
                for tt in range(2):
                    c0 = 2 * P + 2 * HD
                    last = tm(ps[:, gb, tt * 3 * HEADS:(tt + 1) * 3 * HEADS], u.odd,
                              lambda k: slice(c0 + k * 3 * HEADS, c0 + (k + 1) * 3 * HEADS),
                              [(a_hi[:, k, S + tt * P:S + tt * P + P], a_lo[:, k, S + tt * P:S + tt * P + P]) for k in range(KD)])
                last.then_inc(g_ready, 1)
                pe.wait_ge(nsa[j]["gelu_ready"], 2)
                start_product("A", kp)
                N = GROUPS * CS
                fm(ps[:, kb, 0:N], u.odd, 0, [(kg_hi[:, m * N:(m + 1) * N], kg_lo[:, m * N:(m + 1) * N]) for m in range(2)]
                   ).then_inc(k_ready, 1)
                start_product("D", vp)
                for g in range(GROUPS):
                    last = tm(ps[:, vb, g * HD:(g + 1) * HD], u.odd, lambda m: slice(2 * P + m * HD, 2 * P + (m + 1) * HD),
                              [(vg_hi[:, (m * GROUPS + g) * P:(m * GROUPS + g + 1) * P],
                                vg_lo[:, (m * GROUPS + g) * P:(m * GROUPS + g + 1) * P]) for m in range(2)])
                last.then_inc(v_ready, 1)
                drained()
                for b in range(2):
                    for h in range(HEADS):
                        g, r = divmod(h, REP)
                        rows, t = half(g % 2), g // 2 * REP + r
                        c = (b * HEADS + h) * CS
                        last = mm(ps[:, CMP_BANK[g % 2], c:c + CS], q_sb[rows, t, b * P:(b + 1) * P], k_cmp[rows, g, :], True, True)
                last.then_inc(nsa[j]["cmp_scores"], 1)

                def turn_cmp():
                    pe.wait_ge(nsa[j]["cmp_p"], 1)
                    for g in range(GROUPS):
                        for b in range(2):
                            i = 2 * g + b
                            last = nc.tensor.transpose(ps[:, T0 + i // 4, i % 4 * P:i % 4 * P + P],
                                                       p_cmp[:, (b * HEADS + g * REP) * 32:(b * HEADS + g * REP) * 32 + P], ident)
                    last.then_inc(nsa[j]["cmp_t"], 1)
                    pe.wait_ge(nsa[j]["cmp_t_taken"], 2)

                attention(f"nsa{j}", turn_cmp)
                out_operands(f"nsa{j}")
                out_units(parts(a_hi, a_lo))
                mixer_ends()

            def run_moba(_):
                operands()
                a = parts(a_hi, a_lo)
                with cnt.loop(pe, 4, unit=2, A=4, mid=2):
                    fm_unit("AA", a)
                    fm_unit("AA", a)
                for _ in range(4):
                    tm_unit(lambda tt: [(a_hi[:, k, S + tt * P:S + tt * P + P], a_lo[:, k, S + tt * P:S + tt * P + P])
                                        for k in range(KD)], [(0, 0), (1, 0)], KV, KV)
                drained()
                attention("moba0")
                out_operands("moba0")
                out_units(parts(a_hi, a_lo))
                mixer_ends()

            def run_conv(_):
                operands()
                a = parts(a_hi, a_lo)
                with cnt.loop(pe, 4, unit=2, A=2, D=2, mid=2):
                    fm_unit("AD", a)
                    fm_unit("AD", a)
                for _ in range(4):
                    fm_unit("DD", a)
                pe.wait_ge(conv_ready, KD)
                out_units([(by_hi[:, k, :], by_lo[:, k, :]) for k in range(KD)])
                mixer_ends()

            def run_ffn(i):
                operands()
                a = parts(a_hi, a_lo)
                if i == 0:
                    pe.wait_ge(c_ready, 1)
                with cnt.loop(pe, 5, unit=6, A=4, D=4, M=2, mid=4):
                    for _ in range(2):
                        fm_unit("AD", a)
                        fm_unit("AD", a)
                        ada_unit()
                fm_unit("AD", a)
                fm_unit("AD", a)
                n["hid"] += FT
                pe.wait_ge(hid_ready, n["hid"])

                def down():
                    u0, _ = unit(cnt, "")
                    begin(u0)
                    u1, [(bank, p, (ready, _))] = unit(cnt, "D")
                    start_product("D", p)
                    for h, u in enumerate((u0, u1)):
                        if h == 1:
                            begin(u1)
                        xs = [(hid_hi[:, f * S:(f + 1) * S], hid_lo[:, f * S:(f + 1) * S])
                              for f in range(h * HALF_FT, (h + 1) * HALF_FT)]
                        fm(ps[:, bank, 0:S], u.odd, 0, xs, h == 0, h == 1).then_inc(unit_done, 1)

                with cnt.loop(pe, 4, unit=4, D=2):
                    down()
                    down()
                sum_residual()

            def layer_mean(T, cols, sem_ready, first):
                for k in range(KD):
                    wait(pe, sem_ready, first + k + 1)
                    last = mm(ps[:, STAT, 0:T], ones, X[:, k, cols], k == 0, k == KD - 1)
                last.then_inc(mean_sum, 1)
                sum_squares(KD, T)

            def run_enter(_):
                pass

            def run_mla(_):
                operands()
                a = parts(a_hi, a_lo, ALL)
                for _ in range(2):
                    fm_unit("AA", a)
                fm_unit("AA", a)
                fm_unit("AD", a)
                sum_squares(QR, 2 * S)
                sum_squares(KR, 2 * S)
                operands(QR)
                cq = parts(cq_hi, cq_lo, ALL)
                for _ in range(2):
                    fm_unit("AAAA", cq)
                fm_unit("AAAA", cq)
                fm_unit("DDDD", cq)
                operands(KR)
                ckv = parts(ckv_hi, ckv_lo, ALL)
                fm_unit("A" * 8, ckv)
                tm_unit(lambda tt: [(ckv_hi[:, k, tt * P:tt * P + P], ckv_lo[:, k, tt * P:tt * P + P]) for k in range(KR)],
                        [(tt, 512 * c) for tt in range(4) for c in range(2)], D, 512)
                drained()
                pe.wait_ge(rope_ready, QR + 1)
                attention("mla0")
                out_operands("mla0")
                first = cnt.n["D"]
                out_units(parts(a_hi, a_lo, ALL))
                layer_mean(2 * S, ALL, taken["D"], first)

            def run_mlp(i):
                cols, T = (ALL, 2 * S) if i == 0 else (LAT, S)
                operands()
                a = parts(a_hi, a_lo, cols)
                hid0 = n["hid"]

                def quarter(q):
                    for _ in range(4):
                        fm_unit("AA", a)
                    wait(pe, hid_ready, q)
                    for _ in range(4):
                        fm_unit("DD", [(mlp_hi[:, k, 0:T], mlp_lo[:, k, 0:T]) for k in range(KD)])

                with cnt.loop(pe, 4, unit=8, A=8, D=8, mid=8) as i_q:
                    quarter(Num(hid0 + KD, KD, i_q))
                n["hid"] += 4 * KD
                layer_mean(T, cols, x_mixed, n["mean"])
                n["mean"] += KD

            def run_na(_):
                operands()
                for _ in range(4):
                    fm_unit("AA", parts(a_hi, a_lo, LAT))
                for _ in range(4):
                    fm_unit("AA", parts(a_hi, a_lo, ALL))
                for _ in range(4):
                    tm_unit(lambda tt: [(a_hi[:, k, tt * P:tt * P + P], a_lo[:, k, tt * P:tt * P + P]) for k in range(KD)],
                            [(tt, 0) for tt in range(4)], KV, KV)
                drained()
                attention("na0")
                out_operands("na0")
                first = cnt.n["D"]
                out_units(parts(a_hi, a_lo, LAT))
                layer_mean(S, LAT, taken["D"], first)

            pe.wait_ge(small_loaded, 16)
            run = dict(nsa=run_nsa, ffn=run_ffn, moba=run_moba, conv=run_conv, enter=run_enter, mla=run_mla, mlp=run_mlp, na=run_na)
            for stage_name, arg in PROGRAM:
                run[stage_name](arg)

        @block.scalar
        def _(act):
            cnt = Counts()
            n = dict(sq=0, std=0, sum=0, tile=0, mean=0, centered=0, step=0, later=lambda: None)

            def step(ins):
                ins.then_inc(act_step, 1)
                n["step"] += 1

            def split(u):
                if not isinstance(u, Num):
                    u = Num(u)
                width = UNIT_WIDTHS[u.c]
                wait(act, landed[u.odd], (u.half + 1).times(16))
                wait(act, unit_done, u - 1)
                for c in halves(width):
                    nc.scalar.copy(w_hi[:, u.odd, c], stage[:, u.odd, c]).then_inc(hi_split, 1)

            def ahead(u):
                if u.reg is not None or u.c + 2 < U:
                    split(u + 2)

            def later():
                n["later"]()
                n["later"] = lambda: None

            def first_splits():
                u = cnt.n["unit"]
                for i in range(2):
                    if u + i < U:
                        split(u + i)

            def next_unit(rings):
                return unit(cnt, rings)

            def drain(dst, made, rows=slice(0, P), func=None, **kw):
                bank, p, (ready, count) = made
                wait(act, ready, count)
                src = ps[rows, bank, 0:dst.free_size()]
                if len(dst.shape) == 3:
                    src = src.rearrange("p (a b) -> p a b", a=dst.shape[1])
                nc.scalar.activation(dst, src, func or ACT.Copy, **kw).then_inc(taken["A"], 1)

            def squares(nk, src, T, ready):
                for k in range(nk):
                    s_, c = ready(k)
                    wait(act, s_, c)
                    wait(act, sq_used, n["sq"] + k - 1)
                    nc.scalar.activation(t_ring[:, (n["sq"] + k) % 2, 0:T], src(k), ACT.Square).then_inc(sq_ready, 1)
                n["sq"] += nk

            def deviation(T, dim, eps):
                act.wait_ge(sq_used, n["sq"])
                nc.scalar.activation(rstd[:, 0:T], ps[:, STAT, 0:T], ACT.Sqrt, bias=col(eps), scale=1.0 / dim
                                     ).then_inc(std_ready, 1)

            def high_tiles(nk, dst, T):
                for k in range(nk):
                    act.wait_ge(normed, n["tile"] + k + 1)
                    nc.scalar.copy(dst(k), p_ring[:, k % 2, 0:T]).then_inc(norm_hi, 1)
                n["tile"] += nk

            def residual_square(made, x):
                r = cnt.next("res")
                wait(act, taken["D"], made[1] + 1)
                wait(act, res_acc, r - 1)
                nc.scalar.activation(t_ring[:, r.odd, 0:S], x, ACT.Square).then_inc(res_sq, 1)

            def residual_deviation():
                n["sum"] += 1
                act.wait_ge(sum_done, n["sum"])
                nc.scalar.activation(rstd[:, 0:S], ps[:, STAT, 0:S], ACT.Sqrt, bias=col("rms_eps"), scale=1.0 / D
                                     ).then_inc(std_ready, 1)

            def mixer_ends():
                for i in range(4):
                    u, made = next_unit("DD")
                    for m in range(2):
                        residual_square(made[m], X[:, 2 * i + m, LAT])
                    ahead(u)
                skip("M")
                residual_deviation()
                u, _ = next_unit("M")
                n["later"] = lambda: ahead(u)

            def rms_operand():
                if cnt.n["unit"] == 0:
                    first_splits()
                    squares(KD, lambda k: X[:, k, LAT], S, lambda k: (x_loaded, 16))
                    deviation(S, D, "rms_eps")
                high_tiles(KD, lambda k: a_hi[:, k, LAT], S)
                later()

            def layer_norm(cols, T, last=False, next_T=None, next_cols=None):
                n["mean"] += 1
                act.wait_ge(mean_sum, n["mean"])
                nc.scalar.activation(rstd[:, 0:T], ps[:, STAT, 0:T], ACT.Copy, scale=1.0 / D).then_inc(mean_ready, 1)
                c0 = n["centered"]
                squares(KD, lambda k: X[:, k, cols], T, lambda k: (centered, c0 + k + 1))
                n["centered"] += KD
                deviation(T, D, "ln_eps")
                if not last:
                    high_tiles(KD, lambda k: a_hi[:, k, next_cols], next_T)
                later()

            def attention(name, load_bias=None):
                a, items = att[name], ITEMS[name]
                for i in range(len(items) + 3):
                    if i < len(items):
                        act.wait_ge(a["s_taken"], i + 1)
                        for r, (c, _) in enumerate(items[i]["rows"]):
                            last = nc.scalar.activation(p_ring[:, i % 3, c], p_ring[:, i % 3, c], ACT.Exp,
                                                        bias=negmax[:, i % 4, r:r + 1], scale=-1.0,
                                                        accum_out=sums[:, i % 4, r:r + 1])
                        last.then_inc(a["exp_done"], 1)
                        if load_bias and i + 4 < len(items):
                            load_bias(i + 4)
                    b = i - 1
                    if 0 <= b < len(items):
                        act.wait_ge(a["t_ready"], b + 1)
                        if b >= 2:
                            act.wait_ge(a["pv_done"], b - 1)
                        c = items[b]["cols"]
                        nc.scalar.copy(t_ring[:, b % 2, 0:c], ps[:, T0 + b % 2, 0:c]).then_inc(a["t_taken"], 1)
                    b = i - 3
                    if 0 <= b and items[b]["last"]:
                        act.wait_ge(a["pv_done"], b + 1)
                        t = items[b]["tile"]
                        nc.scalar.copy(a_hi[:, t, OUT_TOK[name]], ps[:, O0 + t % 2, 0:OUT_COLS[name]]).then_inc(a["o_hi"], 1)

            def skip(rings, times=1):
                for _ in range(times):
                    u, _ = next_unit(rings)
                    ahead(u)

            def run_nsa(j):
                rms_operand()
                s = nsa[j]
                for kv in range(2):
                    u, made = next_unit("AA")
                    for pair in range(2):
                        drain(k_sb[:, 4 + kv, pair * S:(pair + 1) * S], made[pair])
                    ahead(u)
                act.wait_ge(taken["A"], cnt.n["A"])
                q_spare = q_sb[:, :, S:2 * S].rearrange("p (a e) t -> p a e t", e=2)
                for e in range(2):
                    for to in range(2):
                        act.dma_start(q_spare[half(to), :, e, :],
                                      k_sb[half(e), 4:6, :].rearrange("p a (b t) -> p (a b) t", b=2)).then_inc(s["shifted"], 16)
                for i in range(4):
                    u, made = next_unit("AA")
                    for m in range(2):
                        drain(q_sb[:, 2 * i + m, 0:S], made[m])
                    ahead(u)
                for br in range(2):
                    u, made = next_unit("AA")
                    for pair in range(2):
                        drain(k_sb[:, 2 * br + pair, 0:S], made[pair])
                    ahead(u)
                act.wait_ge(s["blocks"], 8)
                nc.scalar.copy(blk_hi, blk_f).then_inc(s["blocks_hi"], 1)
                skip("DD", 2)
                for i in range(4):
                    u, made = next_unit("A")
                    drain(gel[:, i * GROUPS * CS:(i + 1) * GROUPS * CS], made[0], func=ACT.Gelu_apprx_tanh)
                    ahead(u)
                u, made = next_unit("AAD")
                drain(gate[:, :, :], made[0], func=ACT.Sigmoid)
                drain(k_cmp[:, :, :], made[1])
                ahead(u)
                act.wait_ge(s["cmp_shifted"], 1)
                nc.scalar.activation(cmp_s, cmp_s, ACT.Exp, scale=HD ** -0.5).then_inc(s["cmp_exp"], 1)
                act.wait_ge(s["cmp_t"], 1)
                for b in range(2):
                    nc.scalar.copy(v_sb[:, 2, b * 512:(b + 1) * 512], ps[:, T0 + b, :]).then_inc(s["cmp_t_taken"], 1)
                attention(f"nsa{j}")
                mixer_ends()

            def run_moba(_):
                rms_operand()
                t0 = cnt.n["A"]
                with cnt.loop(act, 4, unit=2, A=4, mid=2):
                    for _ in range(2):
                        u, made = next_unit("AA")
                        for m in range(2):
                            t = made[m][1] - t0
                            drain(qk[:, bass.ds(t.v, 1), 0:S].rearrange("p a t -> p (a t)"), made[m])
                        ahead(u)
                skip("DD", 4)
                attention("moba0")
                mixer_ends()

            def run_conv(_):
                rms_operand()

                def pair():
                    u, made = next_unit("AD")
                    p = made[0][1]
                    wait(act, taken["D"], made[1][1] - 1)
                    drain(p_ring[:, p.odd, 0:S], made[0])
                    ahead(u)

                with cnt.loop(act, 4, unit=2, A=2, D=2, mid=2):
                    pair()
                    pair()
                skip("DD", 4)
                mixer_ends()

            def run_ffn(_):
                rms_operand()

                def gate_up():
                    u, made = next_unit("AD")
                    wait(act, taken["D"], made[1][1] - 1)
                    drain(p_ring[:, made[0][1].odd, 0:S], made[0], func=ACT.Silu)
                    ahead(u)

                with cnt.loop(act, 5, unit=6, A=4, D=4, M=2, mid=4):
                    for _ in range(2):
                        gate_up()
                        gate_up()
                        skip("M")
                gate_up()
                gate_up()
                d0 = cnt.n["D"]

                def down():
                    skip("")
                    u, [made] = next_unit("D")
                    residual_square(made, X[:, bass.ds((made[1] - d0).v, 1), LAT].rearrange("p a t -> p (a t)"))
                    return u

                with cnt.loop(act, 3, unit=4, D=2, res=2):
                    ahead(down())
                    ahead(down())
                ahead(down())
                u = down()
                residual_deviation()
                n["later"] = lambda: ahead(u)

            def run_enter(_):
                if PROGRAM[-1][0] != "enter":
                    high_tiles(KD, lambda k: a_hi[:, k, ALL], 2 * S)
                    later()

            def run_mla(_):
                a0 = cnt.n["A"]
                for i in range(3):
                    u, made = next_unit("AA")
                    for m in range(2):
                        drain(cq_raw[:, 2 * i + m, :] if i < 2 else ckv_raw[:, m, :], made[m])
                    ahead(u)
                u, made = next_unit("AD")
                drain(pe_sb[:, 4, :], made[0])
                ahead(u)
                squares(QR, lambda k: cq_raw[:, k, :], 2 * S, lambda k: (taken["A"], a0 + k + 1))
                deviation(2 * S, Q_RANK, "rms_eps")
                high_tiles(QR, lambda k: cq_hi[:, k, :], 2 * S)
                squares(KR, lambda k: ckv_raw[:, k, :], 2 * S, lambda k: (taken["A"], a0 + QR + k + 1))
                deviation(2 * S, KV_RANK, "rms_eps")
                high_tiles(KR, lambda k: ckv_hi[:, k, :], 2 * S)
                for i in range(3):
                    u, made = next_unit("AAAA")
                    for m in range(4):
                        drain(q_sb[:, 4 * i + m, :] if i < 2 else pe_sb[:, m, :], made[m])
                    ahead(u)
                skip("DDDD")
                u, made = next_unit("A" * 8)
                for h in range(MLA_H):
                    drain(k_sb[:, h, :], made[h])
                ahead(u)
                skip("D" * 8)
                attention("mla0")
                skip("DD", 4)
                layer_norm(ALL, 2 * S, next_T=2 * S, next_cols=ALL)

            def run_mlp(i):
                cols, T = (ALL, 2 * S) if i == 0 else (LAT, S)

                def quarter():
                    for _ in range(4):
                        u, made = next_unit("AA")
                        for m in range(2):
                            wait(act, hid_f, cnt.next("relu") - 1)
                            drain(p_ring[:, made[m][1].odd, 0:T], made[m], func=ACT.Relu)
                        ahead(u)
                    skip("DD", 4)

                with cnt.loop(act, 3, unit=8, A=8, D=8, mid=8, relu=8):
                    quarter()
                quarter()
                layer_norm(cols, T, last=i == 1, next_T=2 * S, next_cols=ALL)

            def run_na(_):
                scaled = sm[:, SMALL["na_bq"]]
                step(nc.scalar.mul(scaled, scaled, HD ** -0.5))
                act.wait_ge(operand, n["tile"])
                act.dma_start(p_ring[:, 0:2, :].rearrange("p a b -> p (a b)"), na_bv).then_inc(bv_loaded, 16)
                act.wait_ge(act_step, n["step"])
                for i in range(4):
                    u, made = next_unit("AA")
                    for m in range(2):
                        drain(q_sb[:, 2 * i + m, LAT], made[m], func=ACT.Identity, scale=HD ** -0.5, bias=col("na_bq", 2 * i + m))
                    ahead(u)
                for i in range(4):
                    u, made = next_unit("AA")
                    for m in range(2):
                        drain(k_sb[:, 2 * i + m, :], made[m], func=ACT.Identity, bias=col("na_bk", 2 * i + m))
                    ahead(u)

                def load_bias(i):
                    h, j = ITEMS["na0"][i]["bias"]
                    act.dma_start(bias_ring[:, i % 4, S:2 * S], na_bias[h, j]).then_inc(bias_loaded[i % 4], 16)

                for i in range(4):
                    load_bias(i)
                skip("DDDD", 4)
                attention("na0", load_bias)
                skip("DD", 4)
                layer_norm(LAT, S, next_T=S, next_cols=LAT)

            act.dma_start(sm[:, :], small).then_inc(small_loaded, 16)
            act.dma_start(X[:, :, LAT], x_t.rearrange("(k p) t -> p k t", p=P)).then_inc(x_loaded, 16)
            act.wait_ge(small_loaded, 16)
            step(nc.scalar.activation(c_act[:, :, :], col("c", 0, 2 * KD).rearrange("p (k s) -> p k s", s=2), ACT.Silu))
            act.wait_ge(act_step, n["step"])
            nc.scalar.copy(c_parts[:, :, 0:2], c_act[:, :, :]).then_inc(c_hi, 1)
            run = dict(nsa=run_nsa, ffn=run_ffn, moba=run_moba, conv=run_conv, enter=run_enter, mla=run_mla, mlp=run_mlp, na=run_na)
            for stage_name, arg in PROGRAM:
                run[stage_name](arg)

        @block.vector
        def _(dve):
            cnt = Counts()
            n = dict(std=0, tile=0, mean=0, step=0, norm=0, last=False, later=lambda: None)
            v = nc.vector

            def step(ins):
                ins.then_inc(dve_step, 1)
                n["step"] += 1

            def sync():
                dve.wait_ge(dve_step, n["step"])

            def minus(out, a, b):
                return v.tensor_tensor(out, a, b.bitcast(F32), ALU.subtract)

            def split(u):
                if not isinstance(u, Num):
                    u = Num(u)
                width = UNIT_WIDTHS[u.c]
                for h, c in enumerate(halves(width)):
                    wait(dve, hi_split, u.times(2) + (h + 1))
                    minus(w_lo[:, u.odd, c], stage[:, u.odd, c], w_hi[:, u.odd, c]).then_inc(lo_split, 1)

            def ahead(u):
                if u.reg is not None or u.c + 2 < U:
                    split(u + 2)

            def later():
                n["later"]()
                n["later"] = lambda: None

            def first_splits():
                u = cnt.n["unit"]
                for i in range(2):
                    if u + i < U:
                        split(u + i)

            def next_unit(rings):
                return unit(cnt, rings)

            def skip(rings, times=1):
                for _ in range(times):
                    u, _ = next_unit(rings)
                    ahead(u)

            def ready(made):
                bank, p, (s_, c) = made
                wait(dve, s_, c)
                return bank

            def ada():
                u, [made] = next_unit("M")
                bank = ready(made)
                p = made[1]
                out = mod_raw[:, bass.ds(p.times(2).v, 2), :]
                v.tensor_copy(out, ps[:, bank, 0:8].rearrange("p (a b) -> p a b", b=4)
                              ).then_inc(taken["M"], 1)
                ahead(u)

            def reciprocal_deviation(T):
                n["std"] += 1
                dve.wait_ge(std_ready, n["std"])
                step(v.reciprocal(rstd[:, 0:T], rstd[:, 0:T]))
                sync()

            def operand_tiles(nk, make, hi, lo, T):
                for k in range(nk + 1):
                    if k < nk:
                        wait(dve, operand, n["tile"] + max(k - 1, 0))
                        make(k, p_ring[:, k % 2, 0:T]).then_inc(normed, 1)
                    if k >= 1:
                        dve.wait_ge(norm_hi, n["tile"] + k)
                        minus(lo(k - 1), p_ring[:, (k - 1) % 2, 0:T], hi(k - 1)).then_inc(operand, 1)
                n["tile"] += nk

            def rms_operand(gain):
                if cnt.n["unit"] == 0:
                    first_splits()
                    reciprocal_deviation(S)
                operand_tiles(KD, lambda k, t: v.scalar_tensor_tensor(t, X[:, k, LAT], gain(k), rstd[:, 0:S], ALU.mult, ALU.mult),
                              lambda k: a_hi[:, k, LAT], lambda k: a_lo[:, k, LAT], S)
                later()

            HALVES = [(CTX, 1), (LAT, 0)]

            def modulate(layer, chunk, cols):
                parts = HALVES if cols == ALL else [(LAT, 0)]
                T = S * len(parts)

                def make(k, t):
                    for i, (c, s_) in enumerate(parts):
                        last = v.tensor_scalar(t[:, i * S:(i + 1) * S], X[:, k, c], mods(layer, chunk + 1, k, s_),
                                               mods(layer, chunk, k, s_), ALU.mult, ALU.add)
                    return last

                operand_tiles(KD, make, lambda k: a_hi[:, k, cols], lambda k: a_lo[:, k, cols], T)

            def layer_norm(cols, T, gname, bname, layer):
                n["mean"] += 1
                dve.wait_ge(mean_ready, n["mean"])
                for k in range(KD):
                    v.tensor_tensor(X[:, k, cols], X[:, k, cols], rstd[:, 0:T], ALU.subtract).then_inc(centered, 1)
                reciprocal_deviation(T)
                for k in range(KD):
                    step(v.tensor_tensor(X[:, k, cols], X[:, k, cols], rstd[:, 0:T], ALU.mult))
                for k in range(KD):
                    dve.wait_ge(dve_step, n["step"] - KD + k + 1)
                    ins = v.tensor_scalar(X[:, k, cols], X[:, k, cols], col(gname, layer * KD + k), col(bname, layer * KD + k),
                                          ALU.mult, ALU.add)
                    ins.then_inc(x_final if n["last"] else x_norm, 1)
                if not n["last"]:
                    n["norm"] += KD
                    dve.wait_ge(x_norm, n["norm"])

            def scale_residual(cols):
                for k in range(KD):
                    step(v.tensor_scalar(X[:, k, cols], X[:, k, cols], ALPHA, None, ALU.mult))

            def add_square():
                r = cnt.next("res")
                wait(dve, res_sq, r + 1)
                wait(dve, res_acc, r)
                v.tensor_tensor(sq_sum, sq_sum, t_ring[:, r.odd, 0:S], ALU.add).then_inc(res_acc, 1)

            def mixer_ends():
                step(v.memset(sq_sum, 0.0))
                sync()
                for i in range(4):
                    u, made = next_unit("DD")
                    for m in range(2):
                        bank = ready(made[m])
                        k = 2 * i + m
                        v.tensor_tensor(X[:, k, LAT], ps[:, bank, 0:S], X[:, k, LAT], ALU.add).then_inc(taken["D"], 1)
                    for m in range(2):
                        add_square()
                    ahead(u)
                ada()
                reciprocal_deviation(S)
                n["later"] = ada

            def gated_residual_units(layer, chunk, cols):
                sync()
                for i in range(4):
                    u, made = next_unit("DD")
                    for m in range(2):
                        bank = ready(made[m])
                        k = 2 * i + m
                        for c, s_ in HALVES if cols == ALL else [(LAT, 0)]:
                            src = ps[:, bank, c] if cols == ALL else ps[:, bank, 0:S]
                            last = v.scalar_tensor_tensor(X[:, k, c], src, mods(layer, chunk, k, s_), X[:, k, c],
                                                          ALU.mult, ALU.add)
                        last.then_inc(taken["D"], 1)
                    ahead(u)

            def attention(name, bias=False):
                a, items = att[name], ITEMS[name]
                tiles = 0
                for i in range(len(items) + 3):
                    if i < len(items):
                        dve.wait_ge(a["s_ready"], i + 1)
                        if i >= 3:
                            dve.wait_ge(a["t_ready"], i - 2)
                        if bias:
                            dve.wait_ge(bias_loaded[i % 4], 16 * (i // 4 + 1))
                        for r, (c, mask) in enumerate(items[i]["rows"]):
                            last = v.tensor_tensor_reduce(p_ring[:, i % 3, c], ps[:, S0 + i % 3, c], mask, NEG_SCALE[name], 3e38,
                                                          ALU.add, ALU.min, negmax[:, i % 4, r:r + 1])
                        last.then_inc(a["s_taken"], 1)
                    b = i - 1
                    if 0 <= b < len(items):
                        w = len(items[b]["rows"])
                        g = items[b]["gate"]
                        dve.wait_ge(a["exp_done"], b + 1)
                        step(v.reciprocal(recip[:, b % 4, 0:w], sums[:, b % 4, 0:w]))
                        if g is not None:
                            sync()
                            step(v.tensor_tensor(recip[:, b % 4, 0:w], recip[:, b % 4, 0:w], gate[:, :, g], ALU.mult))
                        sync()
                        for r, (c, _) in enumerate(items[b]["rows"]):
                            last = v.tensor_scalar(p_ring[:, b % 3, c], p_ring[:, b % 3, c], recip[:, b % 4, r:r + 1], None, ALU.mult)
                        last.then_inc(a["p_ready"], 1)
                    b = i - 3
                    if 0 <= b and items[b]["last"]:
                        tiles += 1
                        dve.wait_ge(a["o_hi"], tiles)
                        t = items[b]["tile"]
                        minus(a_lo[:, t, OUT_TOK[name]], ps[:, O0 + t % 2, 0:OUT_COLS[name]], a_hi[:, t, OUT_TOK[name]]
                              ).then_inc(a["o_ready"], 1)

            def values(rings, unit_col, width, add=None):
                u, made = next_unit(rings)
                for tt, m in enumerate(made):
                    bank = ready(m)
                    dst = v_sb[:, tt, unit_col:unit_col + width]
                    if add is None:
                        ins = v.tensor_copy(dst, ps[:, bank, 0:width])
                    else:
                        ins = v.tensor_tensor(dst, ps[:, bank, 0:width], add, ALU.add)
                    ins.then_inc(taken["D"], 1)
                ahead(u)

            def run_nsa(j):
                rms_operand(lambda k: col("norm_mix", 3 * j * KD + k))
                s = nsa[j]
                skip("AA", 4)
                v_rep = [h.rearrange("p (m g r c) -> p m g r c", m=2, g=GROUPS, r=REP) for h in (vg_hi, vg_lo)]
                step(v.memset(vg_hi.bitcast(F32), 0.0))
                step(v.memset(vg_lo.bitcast(F32), 0.0))
                step(v.memset(p_cmp, 0.0))
                blocks = blk_f.rearrange("p (kv l g c) -> p kv l g c", kv=2, l=16, g=GROUPS)
                step(v.memset(blk_f.rearrange("p (n c) -> p n c", c=CS)[:, :, N_CMP:CS], 0.0))
                dve.wait_ge(s["shifted"], 64)
                for kv in range(2):
                    for par in range(2):
                        src = q_sb[half(par), kv * GROUPS:(kv + 1) * GROUPS, S:2 * S].rearrange("p g (c o) -> p g c o", o=CMP_STRIDE)
                        pos = sm[half(par), SMALL["pos"].start + (j * 2 + kv) * 16:SMALL["pos"].start + (j * 2 + kv) * 16 + 16]
                        for late in range(2):
                            for g in range(GROUPS):
                                at = src[:, g, late:late + N_CMP, par:CMP_STRIDE:2].rearrange("p c l -> p l c")
                                ps_ = pos[:, late * 8:late * 8 + 8].unsqueeze(2).to_broadcast([HD, 8, N_CMP])
                                ins = v.tensor_tensor(blocks[half(par), kv, late * 8:late * 8 + 8, g, 0:N_CMP], at, ps_, ALU.add)
                            ins.then_inc(s["blocks"], 1)
                skip("AA", 4)
                dve.wait_ge(s["blocks_hi"], 1)
                sync()
                minus(blk_lo, blk_f, blk_hi).then_inc(s["blocks_ready"], 1)
                for br in range(2):
                    values("DD", br * KV, KV)
                a0 = cnt.n["A"]
                skip("A", 4)
                u, made = next_unit("AAD")
                N = GROUPS * CS
                dve.wait_ge(taken["A"], a0 + 2)
                step(v.tensor_copy(kg_hi, gel[:, 0:2 * N]))
                sync()
                minus(kg_lo, gel[:, 0:2 * N], kg_hi).then_inc(s["gelu_ready"], 1)
                dve.wait_ge(taken["A"], a0 + 4)
                rep = [gel[:, (2 + m) * N:(3 + m) * N].rearrange("p (g c) -> p g c", g=GROUPS).unsqueeze(2)
                       .to_broadcast([P, GROUPS, REP, CS]) for m in range(2)]
                for m in range(2):
                    step(v.tensor_copy(v_rep[0][:, m, :, :, 0:CS], rep[m]))
                sync()
                for m in range(2):
                    ins = minus(v_rep[1][:, m, :, :, 0:CS], rep[m], v_rep[0][:, m, :, :, 0:CS])
                ins.then_inc(s["gelu_ready"], 1)
                v_blk = v_sb[:, 3, :].rearrange("p (g r d) -> p g r d", g=GROUPS, r=REP)
                dve.wait_ge(s["blocks_ready"], 1)
                step(v.memset(v_sb[:, 3, :], 0.0))
                bank = ready(made[2])
                sync()
                for r in range(REP):
                    rows = slice(32 * r, 32 * r + 32)
                    ins = v.tensor_copy(v_blk[rows, :, r, :], ps[rows, bank, 0:KV].rearrange("p (g d) -> p g d", g=GROUPS))
                ins.then_inc(taken["D"], 1)
                ahead(u)
                dve.wait_ge(s["cmp_scores"], 1)
                rows3 = cmp_s.rearrange("p (n c) -> p n c", c=CS)
                for b in range(2):
                    mask = sm[:, SMALL["cmp_mask"].start + b * CS:SMALL["cmp_mask"].start + (b + 1) * CS]
                    mask = mask.unsqueeze(1).unsqueeze(1).to_broadcast([P, 2, REP, CS])
                    for e in range(2):
                        shape = dict(pair=2, e=2, r=REP)
                        to = cmp_s[:, b * S:(b + 1) * S].rearrange("p (pair e r c) -> p pair e r c", **shape)[:, :, e]
                        of = ps[:, CMP_BANK[e], b * S:(b + 1) * S].rearrange("p (pair e r c) -> p pair e r c", **shape)[:, :, e]
                        step(v.tensor_tensor(to, of, mask, ALU.add))
                sync()
                step(v.tensor_reduce(cmp_max[:, :], rows3, AX_X, ALU.max))
                sync()
                v.tensor_tensor(rows3, rows3, cmp_max[:, :].unsqueeze(2).to_broadcast([P, 2 * HEADS, CS]), ALU.subtract
                                ).then_inc(s["cmp_shifted"], 1)
                dve.wait_ge(s["cmp_exp"], 1)
                step(v.tensor_reduce(cmp_sum[:, :], rows3, AX_X, ALU.add))
                sync()
                step(v.reciprocal(cmp_sum[:, :], cmp_sum[:, :]))
                sync()
                for b in range(2):
                    c = slice(b * HEADS, (b + 1) * HEADS)
                    step(v.scalar_tensor_tensor(cmp_sum[:, c], cmp_sum[:, c], col("valid", b), gate[:, b, 0:HEADS],
                                                ALU.mult, ALU.mult))
                sync()
                v.tensor_tensor(p_cmp.rearrange("p (n c) -> p n c", c=32)[:, :, 0:CS], rows3,
                                cmp_sum[:, :].unsqueeze(2).to_broadcast([P, 2 * HEADS, CS]), ALU.mult).then_inc(s["cmp_p"], 1)
                attention(f"nsa{j}")
                mixer_ends()

            def run_moba(_):
                rms_operand(lambda k: col("norm_mix", KD + k))
                with cnt.loop(dve, 4, unit=2, A=4, mid=2):
                    skip("AA", 2)
                for i in range(4):
                    values("DD", i * KV, KV)
                attention("moba0")
                mixer_ends()

            def run_conv(_):
                rms_operand(lambda k: col("norm_mix", 2 * KD + k))
                d0 = cnt.n["D"]

                def product():
                    u, made = next_unit("AD")
                    bank = ready(made[1])
                    wait(dve, taken["A"], made[0][1] + 1)
                    f = made[1][1] - d0
                    v.tensor_tensor(conv_z[:, bass.ds(f.v, 1), :].rearrange("p a t -> p (a t)"), ps[:, bank, 0:S],
                                    p_ring[:, made[0][1].odd, 0:S], ALU.mult).then_inc(taken["D"], 1)
                    ahead(u)

                with cnt.loop(dve, 4, unit=2, A=2, D=2, mid=2):
                    product()
                    product()
                dve.wait_ge(taken["D"], cnt.n["D"])
                for i in range(4):
                    u, made = next_unit("DD")
                    for m in range(2):
                        k = 2 * i + m
                        y = t_ring[:, k % 2, 0:S]
                        wait(dve, conv_ready, k - 1)
                        w = [col("conv_w", j * KD + k) for j in range(3)]
                        z = conv_z[:, k, :]
                        step(v.tensor_scalar(y, z, w[2], None, ALU.mult))
                        sync()
                        step(v.scalar_tensor_tensor(y[:, 1:S], z[:, 0:S - 1], w[1], y[:, 1:S], ALU.mult, ALU.add))
                        sync()
                        step(v.scalar_tensor_tensor(y[:, 2:S], z[:, 0:S - 2], w[0], y[:, 2:S], ALU.mult, ALU.add))
                        sync()
                        bank = ready(made[m])
                        v.tensor_tensor(y, ps[:, bank, 0:S], y, ALU.mult).then_inc(taken["D"], 1)
                        dve.wait_ge(taken["D"], made[m][1].c + 1)
                        v.tensor_copy(by_hi[:, k, :], y).then_inc(conv_hi, 1)
                        dve.wait_ge(conv_hi, k + 1)
                        minus(by_lo[:, k, :], y, by_hi[:, k, :]).then_inc(conv_ready, 1)
                    ahead(u)
                mixer_ends()

            def run_ffn(i):
                rms_operand(lambda k: col("norm_ffn", i * KD + k))
                h0 = cnt.n["hid"]

                def gate_up():
                    u, made = next_unit("AD")
                    h = cnt.next("hid")
                    wait(dve, taken["A"], made[0][1] + 1)
                    bank = ready(made[1])
                    y = t_ring[:, h.odd, 0:S]
                    v.tensor_tensor(y, ps[:, bank, 0:S], p_ring[:, made[0][1].odd, 0:S], ALU.mult).then_inc(taken["D"], 1)
                    wait(dve, taken["D"], made[1][1] + 1)
                    c = bass.ds((h - h0).times(S).v, S)
                    v.tensor_copy(hid_hi[:, c], y).then_inc(hid_h, 1)
                    wait(dve, hid_h, h + 1)
                    minus(hid_lo[:, c], y, hid_hi[:, c]).then_inc(hid_ready, 1)
                    ahead(u)
                    wait(dve, hid_ready, h + 1)

                with cnt.loop(dve, 5, unit=6, A=4, D=4, M=2, mid=4, hid=4):
                    for _ in range(2):
                        gate_up()
                        gate_up()
                        ada()
                gate_up()
                gate_up()
                d0 = cnt.n["D"]

                step(v.memset(sq_sum, 0.0))
                sync()

                def down(last=False):
                    u0, _ = next_unit("")
                    if not last:
                        ahead(u0)
                    u1, [made] = next_unit("D")
                    bank = ready(made)
                    k = bass.ds((made[1] - d0).v, 1)
                    x = X[:, k, LAT].rearrange("p a t -> p (a t)")
                    v.tensor_tensor(x, ps[:, bank, 0:S], x, ALU.add).then_inc(taken["D"], 1)
                    if last:
                        add_square()
                        ahead(u0)
                        n["later"] = lambda: ahead(u1)
                    else:
                        ahead(u1)
                        add_square()

                with cnt.loop(dve, 3, unit=4, D=2, res=2):
                    down()
                    down()
                down()
                down(True)
                reciprocal_deviation(S)

            def run_enter(_):
                for k in range(KD):
                    v.scalar_tensor_tensor(X[:, k, LAT], X[:, k, LAT], col("norm_final", k), rstd[:, 0:S], ALU.mult, ALU.mult
                                           ).then_inc(x_final if n["last"] else x_norm, 1)
                if n["last"]:
                    return
                n["norm"] += KD
                dve.wait_ge(ctx_loaded, 16)
                dve.wait_ge(taken["M"], MOD_TILES // 2)
                step(v.tensor_copy(mod[:, :, :], mod_raw[:, :, 0:2]))
                sync()
                step(v.tensor_tensor(mod[:, :, :], mod[:, :, :], mod_raw[:, :, 2:4], ALU.add))
                sync()
                step(v.tensor_tensor(mod[:, :, :], mod[:, :, :], col("ada_b", 0, MOD_TILES).unsqueeze(2).to_broadcast([P, MOD_TILES, 2]),
                                     ALU.add))
                sync()
                for layer in range(2):
                    for chunk in (1, 4):
                        j = (layer * ADA_CHUNKS + chunk) * KD
                        step(v.tensor_scalar(mod[:, j:j + KD, :], mod[:, j:j + KD, :], 1.0, None, ALU.add))
                sync()
                dve.wait_ge(x_norm, n["norm"])
                modulate(0, 0, ALL)
                later()

            def rope(dst, made, done):
                turned = p_ring[:, 0, 0:S]
                bank = ready(made)
                v.tensor_tensor(turned, ps[:, bank, LAT], col("sin", 0, S), ALU.mult).then_inc(taken["D"], 1)
                step(v.tensor_tensor(dst[:, LAT], dst[:, LAT], col("cos", 0, S), ALU.mult))
                sync()
                dve.wait_ge(taken["D"], made[1].c + 1)
                v.tensor_tensor(dst[:, LAT], dst[:, LAT], turned, ALU.add).then_inc(rope_ready, 1)
                dve.wait_ge(rope_ready, done)

            def run_mla(_):
                scale_residual(ALL)
                skip("AA", 3)
                u, made = next_unit("AD")
                dve.wait_ge(taken["A"], cnt.n["A"])
                rope(pe_sb[:, 4, :], made[1], 1)
                ahead(u)
                for raw, gain, nk, hi, lo in ((cq_raw, "q_norm", QR, cq_hi, cq_lo), (ckv_raw, "kv_norm", KR, ckv_hi, ckv_lo)):
                    reciprocal_deviation(2 * S)
                    operand_tiles(nk, lambda k, t: v.scalar_tensor_tensor(t, raw[:, k, :], col(gain, k), rstd, ALU.mult, ALU.mult),
                                  lambda k: hi[:, k, :], lambda k: lo[:, k, :], 2 * S)
                skip("AAAA", 3)
                a_end = cnt.n["A"]
                u, made = next_unit("DDDD")
                for m in range(4):
                    dve.wait_ge(taken["A"], a_end - 4 + m + 1)
                    rope(pe_sb[:, m, :], made[m], m + 2)
                ahead(u)
                skip("A" * 8)
                u, made = next_unit("D" * 8)
                for i, m in enumerate(made):
                    bank = ready(m)
                    tt, c = divmod(i, 2)
                    v.tensor_copy(v_sb[:, tt, 512 * c:512 * c + 512], ps[:, bank, :]).then_inc(taken["D"], 1)
                ahead(u)
                attention("mla0")
                gated_residual_units(0, 2, ALL)
                layer_norm(ALL, 2 * S, "ln1_g", "ln1_b", 0)
                modulate(0, 3, ALL)

            def run_mlp(i):
                cols, T = (ALL, 2 * S) if i == 0 else (LAT, S)
                scale_residual(cols)
                for k in range(KD):
                    ins = v.memset(y_acc[:, k, 0:T], 0.0)
                    if i == 0 and k < 2:
                        ins.then_inc(hid_f, 1)
                    else:
                        step(ins)
                sync()
                if i == 0:
                    dve.wait_ge(hid_f, 2)

                def quarter():
                    for q in range(4):
                        u, made = next_unit("AA")
                        for m in range(2):
                            wait(dve, taken["A"], made[m][1] + 1)
                            k = 2 * q + m
                            r, h = cnt.next("relu"), cnt.next("hid")
                            y = t_ring[:, r.odd, 0:T]
                            x = p_ring[:, made[m][1].odd, 0:T]
                            v.tensor_tensor(y, x, x, ALU.mult).then_inc(hid_f, 1)
                            wait(dve, hid_f, r + 1)
                            v.tensor_copy(mlp_hi[:, k, 0:T], y).then_inc(hid_h, 1)
                            wait(dve, hid_h, h + 1)
                            minus(mlp_lo[:, k, 0:T], y, mlp_hi[:, k, 0:T]).then_inc(hid_ready, 1)
                        ahead(u)
                        wait(dve, hid_ready, h + 1)
                    for q in range(4):
                        u, made = next_unit("DD")
                        for m in range(2):
                            bank = ready(made[m])
                            k = 2 * q + m
                            v.tensor_tensor(y_acc[:, k, 0:T], ps[:, bank, 0:T], y_acc[:, k, 0:T], ALU.add).then_inc(taken["D"], 1)
                        ahead(u)

                with cnt.loop(dve, 3, unit=8, A=8, D=8, mid=8, relu=8, hid=8):
                    quarter()
                quarter()
                dve.wait_ge(taken["D"], cnt.n["D"])
                for k in range(KD):
                    for c, s_ in HALVES if i == 0 else [(LAT, 0)]:
                        y = y_acc[:, k, c] if i == 0 else y_acc[:, k, 0:S]
                        last = v.scalar_tensor_tensor(X[:, k, c], y, mods(i, 5, k, s_), X[:, k, c], ALU.mult, ALU.add)
                    last.then_inc(x_mixed, 1)
                layer_norm(cols, T, "ln2_g", "ln2_b", i)
                if i == 0:
                    modulate(1, 0, ALL)

            def run_na(_):
                scale_residual(LAT)
                step(v.memset(bias_ring[:, 0:4, 0:S], 0.0))
                skip("AA", 8)
                dve.wait_ge(bv_loaded, 16)
                bv = p_ring[:, 0:2, :].rearrange("p a b -> p (a b)")
                for i in range(4):
                    values("DDDD", i * KV, KV, bv[:, i * KV:(i + 1) * KV])
                sync()
                attention("na0", bias=True)
                gated_residual_units(1, 2, LAT)
                layer_norm(LAT, S, "ln1_g", "ln1_b", 1)
                modulate(1, 3, LAT)

            dve.wait_ge(small_loaded, 16)
            dve.wait_ge(c_hi, 1)
            minus(c_parts[:, :, 2:4], c_act[:, :, :], c_parts[:, :, 0:2]).then_inc(c_ready, 1)
            run = dict(nsa=run_nsa, ffn=run_ffn, moba=run_moba, conv=run_conv, enter=run_enter, mla=run_mla, mlp=run_mlp, na=run_na)
            for at, (stage_name, arg) in enumerate(PROGRAM):
                n["last"] = at == len(PROGRAM) - 1
                run[stage_name](arg)


def _tiles(w, kt, mt):
    m = w.shape[1] // (P * mt)
    t = w.reshape(kt, P, m, mt, P).transpose(2, 1, 3, 0, 4)
    return list(t.reshape(m, P, kt * mt * P))


def _cols(w, width):
    kt, m = w.shape[0] // P, w.shape[1] // width
    return list(w.reshape(kt, P, m, width).transpose(2, 1, 0, 3).reshape(m, P, kt * width))


def _units(i):
    cat = np.concatenate
    ada = cat([np.asarray(i["ada_w_2"][layer]) for layer in range(2)], axis=1)
    ada = iter(_tiles(ada, KD, 2))
    heads = [(2 * pair + e) * REP + r for pair in range(2) for r in range(REP) for e in range(2)]
    head_cols = np.concatenate([np.arange(h * HD, (h + 1) * HD) for h in heads])
    swap = np.arange(ROPE) ^ 16
    for stage_name, j in PROGRAM:
        if stage_name == "nsa":
            w = i["nsa_w_in"][j]
            q = HEADS * HD
            parts = [w[:, q + n * KV:q + (n + 1) * KV] for n in range(6)]
            yield from _tiles(parts[0], KD, 2)
            yield from _tiles(parts[1], KD, 2)
            yield from _tiles(w[:, head_cols], KD, 2)
            yield from _tiles(parts[2], KD, 2)
            yield from _tiles(parts[4], KD, 2)
            yield from _cols(parts[3], KV)
            yield from _cols(parts[5], KV)
            yield from _tiles(i["nsa_cmp_k_w1"][j], 16, 1)
            yield from _tiles(i["nsa_cmp_v_w1"][j], 16, 1)
            k2 = i["nsa_cmp_k_w2"][j]
            yield cat([*_tiles(cat([k2, k2], axis=1), 2, 1), *_cols(i["nsa_cmp_v_w2"][j], HD),
                       *_cols(w[:, q + 6 * KV:], 3 * HEADS)], axis=1)
            yield from _tiles(i["nsa_w_out"][j][head_cols], KD, 2)
            yield next(ada)
            yield next(ada)
        elif stage_name == "moba":
            w = i["moba_w_in"][j]
            yield from _tiles(w[:, 0:2 * D], KD, 2)
            yield from _cols(w[:, 2 * D:], KV)
            yield from _tiles(i["moba_w_out"][j], KD, 2)
            yield next(ada)
            yield next(ada)
        elif stage_name == "conv":
            w = i["conv_w_in"][j]
            c, u = w[:, D:2 * D].reshape(D, KD, 1, P), w[:, 2 * D:].reshape(D, KD, 1, P)
            yield from _tiles(cat([c, u], axis=2).reshape(D, 2 * D), KD, 2)
            yield from _tiles(w[:, 0:D], KD, 2)
            yield from _tiles(i["conv_w_out"][j], KD, 2)
            yield next(ada)
            yield next(ada)
        elif stage_name == "ffn":
            g, u = (i[n][j].reshape(D, FT, 1, P) for n in ("ffn_w_gate", "ffn_w_up"))
            pairs = iter(_tiles(cat([g, u], axis=2).reshape(D, 2 * D_FF), KD, 2))
            for _ in range(10):
                yield next(pairs)
                yield next(pairs)
                yield next(ada)
            yield next(pairs)
            yield next(pairs)
            w = i["ffn_w_down"][j].reshape(2, HALF_FT, P, KD, P).transpose(3, 0, 2, 1, 4)
            yield from w.reshape(2 * KD, P, HALF_FT * P)
        elif stage_name == "mla":
            yield from _tiles(i["mla_w_dq_2"][0], KD, 2)
            w = i["mla_w_dkv_2"][0]
            pe = w[:, KV_RANK:]
            yield from _tiles(w[:, 0:KV_RANK], KD, 2)
            yield from _tiles(cat([pe, pe, pe[:, swap], pe[:, swap]], axis=1), KD, 2)
            w = i["mla_w_uq_2"][0].reshape(Q_RANK, MLA_H, NOPE + ROPE)
            pe = w[:, :, NOPE:]
            yield from _tiles(w[:, :, 0:NOPE].reshape(Q_RANK, -1), QR, 4)
            yield from _tiles(pe.reshape(Q_RANK, -1), QR, 4)
            yield from _tiles(pe[:, :, swap].reshape(Q_RANK, -1), QR, 4)
            w = i["mla_w_ukv_2"][0].reshape(KV_RANK, MLA_H, NOPE + MLA_V)
            yield from _tiles(w[:, :, 0:NOPE].reshape(KV_RANK, -1), KR, 8)
            yield from _cols(w[:, :, NOPE:].reshape(KV_RANK, -1), D)
            yield from _tiles(i["mla_w_o_2"][0], KD, 2)
        elif stage_name == "na":
            w = i["na_w_qkv_2"][0]
            yield from _tiles(w[:, 0:2 * D], KD, 2)
            yield from _cols(w[:, 2 * D:], KV)
            yield from _tiles(i["na_w_o_2"][0], KD, 2)
        elif stage_name == "mlp":
            up = _tiles(i["mlp_w1_2"][j], KD, 2)
            down = [u for q in range(4) for u in _tiles(i["mlp_w2_2"][j][q * D:(q + 1) * D], KD, 2)]
            for q in range(4):
                yield from up[4 * q:4 * q + 4]
                yield from down[4 * q:4 * q + 4]


def _features(a):
    a = np.asarray(a)
    return a.reshape(-1, P).T


def _small(i):
    s = np.zeros((P, N_SMALL), np.float32)

    def put(name, a):
        s[:, SMALL[name]] = a

    for name, key in [("norm_mix", "norm_mix"), ("norm_ffn", "norm_ffn"), ("norm_final", "norm_final"), ("ada_b", "ada_b_2"),
                      ("ln1_g", "ln1_g_2"), ("ln1_b", "ln1_b_2"), ("ln2_g", "ln2_g_2"), ("ln2_b", "ln2_b_2"),
                      ("q_norm", "mla_q_norm_2"), ("kv_norm", "mla_kv_norm_2"), ("conv_w", "conv_w")]:
        put(name, _features(i[key]))
    put("c", np.stack([_features(i["c_2"]), _features(i["c_ctx_2"])], axis=2).reshape(P, 2 * KD))
    b = np.asarray(i["na_b_qkv_2"][0])
    put("na_bq", _features(b[0:D]))
    put("na_bk", _features(b[D:2 * D]))
    pos = np.stack([i["nsa_cmp_pos_k"], i["nsa_cmp_pos_v"]], axis=1)
    put("pos", pos.reshape(2, 2, CMP_BLOCK // 2, 2 * HD).transpose(3, 0, 1, 2).reshape(P, -1))
    put("rms_eps", RMS_EPS)
    put("ln_eps", LN_EPS)
    q = np.arange(P)[:, None] + P * np.arange(2)[None, :]
    put("valid", q >= CMP_BLOCK - 1)
    c = np.arange(CS)
    seen = (c * CMP_STRIDE + CMP_BLOCK - 1 <= q[:, :, None]) & (c < N_CMP)
    put("cmp_mask", np.where(seen, 0.0, NEG).reshape(P, -1))
    p = np.arange(P)
    put("causal", np.concatenate([np.zeros((P, P)), np.where(p[None, :] <= p[:, None], 0.0, NEG)], axis=1))
    put("ident", np.eye(P))
    put("ones", 1.0)
    d = p % ROPE
    t = np.arange(S)
    pos = np.where((d < ROPE // 2)[:, None], t // GRID_W, t % GRID_W).astype(np.float32)
    n = ROPE // 4
    freqs = np.power(np.float32(ROPE_THETA), -(np.arange(n, dtype=np.float32) / np.float32(n))).astype(np.float32)
    ang = pos * freqs[d % n][:, None]
    put("cos", np.cos(ang))
    put("sin", np.sin(ang) * np.where(d % (2 * n) < n, -1.0, 1.0)[:, None].astype(np.float32))
    return s


def _na_bias(rpb):
    t = np.arange(S)
    r, c = t // GRID_W, t % GRID_W
    start = np.clip(c - NA_COLS // 2, 0, GRID_W - NA_COLS)
    seen = (c[None, :] >= start[:, None]) & (c[None, :] < start[:, None] + NA_COLS)
    dr = r[None, :] - r[:, None] + NA_ROWS - 1
    dc = np.clip(c[None, :] - c[:, None] + NA_COLS - 1, 0, 2 * NA_COLS - 2)
    bias = np.asarray(rpb)[:, dr, dc]
    bias[:, ~seen] = NEG
    return bias.reshape(HEADS, 2, P, S)


def kernel(**inputs):
    import concourse.bacc as bacc
    from concourse.bass_utils import run_bass_kernel_spmd as run

    i = {k: np.asarray(a) for k, a in inputs.items()}
    weights = np.zeros((P, U, UC), np.float32)
    for u, part in enumerate(_units(i)):
        assert part.shape == (P, UNIT_WIDTHS[u]), (u, part.shape, UNIT_WIDTHS[u])
        weights[:, u, 0:part.shape[1]] = part
    assert u == U - 1, (u, U)
    arrays = {
        "weights": weights.reshape(P, U * UC),
        "small": _small(i),
        "x_t": np.ascontiguousarray(i["x"][0].T),
        "ctx_t": np.ascontiguousarray(i["ctx_2"][0].T),
        "na_bias": np.ascontiguousarray(_na_bias(i["na_rpb_2"][0])),
        "na_bv": np.ascontiguousarray(np.broadcast_to(i["na_b_qkv_2"][0][2 * D:], (P, D))),
    }
    nc = bacc.Bacc("TRN2", target_bir_lowering=False, num_devices=1, dynamic_dma_scratch_size=1024)
    args = [nc.dram_tensor(name, a.shape, F32, kind="ExternalInput").ap() for name, a in arrays.items()]
    out = nc.dram_tensor("out_t", (D, S), F32, kind="ExternalOutput").ap()
    program(nc, *args, out)
    got = run(nc, [arrays], core_ids=[0])
    return np.ascontiguousarray(got.results[0]["out_t"].T).reshape(1, S, D)
```

```python
from contextlib import ExitStack, contextmanager

import concourse.bass as bass
from concourse import mybir
from concourse.alu_op_type import AluOpType as ALU
import numpy as np

ACT = mybir.ActivationFunctionType
F32 = mybir.dt.float32
F32R = mybir.dt.float32r
AX_X = mybir.AxisListType.X

P = 128
D = 1024
S = 256
KD = D // P
HD = 64
GROUPS, REP, HEADS = 4, 4, 16
KV = GROUPS * HD
CMP_BLOCK, CMP_STRIDE = 32, 16
N_CMP = (S - CMP_BLOCK) // CMP_STRIDE + 1
CS = 16
D_FF = -(-8 * D // (3 * 256)) * 256
FT = D_FF // P
MLA_H, NOPE, ROPE, MLA_V, Q_RANK, KV_RANK = 8, 128, 64, 128, 512, 256
QR, KR = Q_RANK // P, KV_RANK // P
GRID_W = 64
NA_ROWS, NA_COLS = 8, 16
ROPE_THETA = 10000.0
RMS_EPS, LN_EPS = 1e-6, 1e-5
ALPHA = float(np.float32((2.0 * 2) ** 0.25))
NEG = -1e30
ADA_CHUNKS = 6
MOD_TILES = 2 * ADA_CHUNKS * KD

LAT = slice(S, 2 * S)
CTX = slice(0, S)
ALL = slice(0, 2 * S)

TILES = 16
UC = TILES * P
HALF_FT = FT // 2
SMALL_UNIT = 2 * P + 2 * HD + KD * 3 * HEADS

PROGRAM = [("nsa", 0), ("ffn", 0), ("moba", 0), ("ffn", 1), ("conv", 0), ("ffn", 2), ("nsa", 1), ("ffn", 3),
           ("enter", 0), ("mla", 0), ("mlp", 0), ("na", 0), ("mlp", 1)]
WIDTHS = {
    "nsa": [UC] * 14 + [SMALL_UNIT] + [UC] * 4,
    "moba": [UC] * 16,
    "conv": [UC] * 16,
    "ffn": [UC] * FT + [HALF_FT * P] * 2 * KD,
    "enter": [],
    "mla": [UC] * 14,
    "na": [UC] * 16,
    "mlp": [UC] * 32,
}
UNIT_WIDTHS = [w for stage, _ in PROGRAM for w in WIDTHS[stage]]
U = len(UNIT_WIDTHS)


ADA_AT_DOWN = (1, 3, 4, 5)


def _stream():
    stream, u, ada = [("weights", 0), ("weights", 1)], 0, 0
    for stage, _ in PROGRAM:
        for j in range(len(WIDTHS[stage])):
            if u + 2 < U:
                stream.append(("weights", u + 2))
            u += 1
            if stage == "ffn" and (j < FT - 2 or j in [FT + 2 * k + 1 for k in ADA_AT_DOWN]):
                stream.append(("ada", ada))
                ada += 1
    return stream, ada


STREAM, ADA_UNITS = _stream()
STREAM_WIDTHS = [UNIT_WIDTHS[n] if kind == "weights" else D for kind, n in STREAM]


def repeats(keys, start, period):
    n = 1
    while keys[start + n * period:start + (n + 1) * period] == keys[start:start + period]:
        n += 1
    return n


SMALL = {}
_at = 0
for _name, _width in [
    ("norm_mix", 4 * KD), ("norm_ffn", 4 * KD), ("norm_final", KD), ("ada_b", MOD_TILES),
    ("ln1_g", 2 * KD), ("ln1_b", 2 * KD), ("ln2_g", 2 * KD), ("ln2_b", 2 * KD), ("q_norm", QR), ("kv_norm", KR),
    ("na_bq", KD), ("na_bk", KD), ("conv_w", 3 * KD), ("pos", 2 * 2 * CMP_BLOCK // 2), ("rms_eps", 1), ("ln_eps", 1),
    ("zero", 1), ("valid", 2), ("cmp_mask", 2 * CS), ("causal", 2 * P), ("ident", P), ("ones", P),
    ("cos", S), ("sin", S),
]:
    SMALL[_name] = slice(_at, _at + _width)
    _at += _width
N_SMALL = _at


class Num:

    def __init__(self, c, stride=0, reg=None):
        self.c, self.stride, self.reg = c, stride, reg

    def __add__(self, n):
        return Num(self.c + n, self.stride, self.reg)

    def __sub__(self, n):
        return self + -n

    @property
    def v(self):
        return self.c if self.reg is None else self.reg * self.stride + self.c

    @property
    def odd(self):
        return self.c % 2

    @property
    def half(self):
        return Num(self.c // 2, self.stride // 2, self.reg)

    def times(self, n):
        return Num(self.c * n, self.stride * n, self.reg)


class Counts:

    def __init__(self):
        self.n = {"unit": 0, "ada": 0, "A": 0, "D": 0, "mid": 0, "hid": 0, "relu": 2, "res": 0}
        self.reg, self.per = None, {}

    def next(self, name):
        self.n[name] += 1
        return Num(self.n[name] - 1, self.per.get(name, 0), self.reg)

    def peek(self, name):
        return Num(self.n[name], self.per.get(name, 0), self.reg)

    @contextmanager
    def loop(self, eng, times, **per):
        before = dict(self.n)
        with eng.Fori(0, times) as i:
            self.reg, self.per = i, per
            yield i
            assert self.n == {k: v + per.get(k, 0) for k, v in before.items()}, (before, self.n, per)
        self.reg, self.per = None, {}
        self.n = {k: v + times * per.get(k, 0) for k, v in before.items()}


def halves(width):
    cut = -(-width // (2 * P)) * P
    return slice(0, cut), slice(cut, width)


def program(nc, weights, small, x_t, c_rows, ctx_t, na_bias, na_bv, out_t):
    with ExitStack() as ctx:
        def sem(name):
            return ctx.enter_context(nc.semaphore(name))

        def sb(name, shape, dt=F32):
            return ctx.enter_context(nc.sbuf_tensor(name, shape, dt))

        stage = sb("stage", [P, 2, UC])
        w_hi = sb("w_hi", [P, 2, UC], F32R)
        w_lo = sb("w_lo", [P, 2, UC], F32R)
        X = sb("X", [P, KD, 2 * S])
        a_hi = sb("a_hi", [P, KD, 2 * S], F32R)
        a_lo = sb("a_lo", [P, KD, 2 * S], F32R)
        hid_hi = sb("hid_hi", [P, FT * S], F32R)
        hid_lo = sb("hid_lo", [P, FT * S], F32R)
        qk = sb("qk", [P, 2 * KD, 2 * S])
        v_sb = sb("v_sb", [P, 4, D])
        pe_sb = sb("pe_sb", [P, 5, 2 * S])
        p_ring = sb("p_ring", [P, 3, 2 * S])
        t_ring = sb("t_ring", [P, 2, 2 * S])
        sm = sb("sm", [P, N_SMALL])
        mod = sb("mod", [P, MOD_TILES, 2])
        mod_sum = sb("mod_sum", [P, 2, 2])
        gate = sb("gate", [P, 2, 3 * HEADS])
        k_cmp = sb("k_cmp", [P, GROUPS, CS])
        negmax = sb("negmax", [P, 4, 2])
        sums = sb("sums", [P, 4, 2])
        recip = sb("recip", [P, 4, 2])
        mod_g, mod_b = sb("mod_g", [P, KD, 2]), sb("mod_b", [P, KD, 2])
        alpha_g, alpha_b = sb("alpha_g", [P, KD]), sb("alpha_b", [P, KD])
        spare = sb("spare", [P, 1])
        stat = sb("stat", [P, S // P])
        cmp_max = sb("cmp_max", [P, 2 * HEADS])
        cmp_sum = sb("cmp_sum", [P, 2 * HEADS])

        q_sb, k_sb = qk[:, 0:KD], qk[:, KD:2 * KD]
        sq_sum = p_ring[:, 0, 0:S]
        rstd = p_ring[:, 2, :]
        y_acc = q_sb

        ps = ctx.enter_context(nc.psum_tensor("ps", [P, 8, 512], F32))
        BANK = {"A": 0, "D": 2}
        products = ps[:, 5:7, :].rearrange("p a (b n) -> p (a b) n", n=S)
        STAT, S0, T0, O0 = 7, 0, 3, 5
        CMP_BANK = (7, 4)

        def col(name, i=0, n=1):
            return sm[:, SMALL[name].start + i:SMALL[name].start + i + n]

        ident, ones = col("ident", 0, P), col("ones", 0, P)

        small_loaded, x_loaded = sem("small_loaded"), sem("x_loaded")
        landed = [sem("landed0"), sem("landed1")]
        hi_split = sem("hi_split")
        lo_split, lo_rest = sem("lo_split"), sem("lo_rest")
        unit_done = sem("unit_done")
        mid_ready = sem("mid_ready")
        taken = {r: sem(f"taken_{r}") for r in "AD"}
        c_loaded, ada_landed = sem("c_loaded"), [sem("ada_landed0"), sem("ada_landed1")]
        ada_sum, mod_ready = sem("ada_sum"), sem("mod_ready")
        sq_ready, sq_used = sem("sq_ready"), sem("sq_used")
        res_sq, res_acc, sum_done = sem("res_sq"), sem("res_acc"), sem("sum_done")
        std_ready, mean_ready, mean_sum = sem("std_ready"), sem("mean_ready"), sem("mean_sum")
        recip_ready, spread_done = sem("recip_ready"), sem("spread_done")
        centered, x_mixed, x_norm = sem("centered"), sem("x_mixed"), sem("x_norm")
        normed, norm_hi, operand = sem("normed"), sem("norm_hi"), sem("operand")
        hid_f, hid_h, hid_ready = sem("hid_f"), sem("hid_h"), sem("hid_ready")
        dve_step, act_step = sem("dve_step"), sem("act_step")
        att = {n: {e: sem(f"{n}_{e}") for e in ("s_ready", "s_taken", "exp_done", "p_ready", "t_ready",
                                                "t_taken", "pv_done", "o_hi", "o_ready")}
               for n in ("nsa0", "nsa1", "moba0", "mla0", "na0")}
        nsa = [{e: sem(f"{e}{j}") for e in ("shifted", "blocks", "blocks_hi", "blocks_ready", "gelu", "gelu_ready", "cmp_scores",
                                            "cmp_shifted", "cmp_exp", "cmp_p", "cmp_t", "cmp_t_taken")}
               for j in range(2)]
        conv_hi, conv_ready = sem("conv_hi"), sem("conv_ready")
        ctx_loaded, rope_ready = sem("ctx_loaded"), sem("rope_ready")
        bias_loaded = [sem(f"bias_loaded{i}") for i in range(4)]
        bv_loaded, stored, x_final = sem("bv_loaded"), sem("stored"), sem("x_final")

        def wait(eng, s, n):
            if isinstance(n, Num):
                if n.reg is not None:
                    assert n.c > 0
                    eng.wait_ge(s, n.v)
                    return
                n = n.c
            if n > 0:
                eng.wait_ge(s, n)

        def unit(cnt, rings):
            u, made = cnt.next("unit"), []
            for j, ring in enumerate(rings):
                p = cnt.next(ring)
                last = j == len(rings) - 1
                made.append((BANK[ring] + p.odd, p,
                             (unit_done, u + 1) if last else (mid_ready, cnt.next("mid") + 1)))
            return u, made

        def causal_item(tile, q_rows, q, k_tile, v_of, out_rows, first, last, r_of=None, cmp=None):
            kk = k_sb[q_rows, k_tile, 0:S]
            return dict(
                tile=tile, last=last, cols=3 * P, gate=r_of,
                scores=[(slice(0, P), [(q[:, 0:P], kk[:, 0:P])]), (slice(P, 3 * P), [(q[:, P:S], kk)])],
                rows=[(slice(0, P), col("causal", P, P)), (slice(P, 3 * P), col("causal", 0, 2 * P))],
                turns=[(0, 0), (P, P), (2 * P, 2 * P)],
                pv=([(cmp[0], cmp[1], slice(0, S), out_rows)] if cmp else [])
                + [(v_of(0), slice(0, S), slice(0, S), out_rows), (v_of(1), slice(S, S + P), slice(P, S), out_rows)],
                first=first)

        def half(e):
            return slice(HD * e, HD * e + HD)

        def nsa_items():
            items = []
            for pair in range(2):
                for r in range(REP):
                    for e in range(2):
                        g = 2 * pair + e
                        h = g * REP + r
                        for br in range(2):
                            cmp = None
                            if br == 0:
                                cmp = (v_sb[:, 3, (g * REP + r) * HD:(g * REP + r + 1) * HD],
                                       v_sb[:, 2, g * S:(g + 1) * S])
                            items.append(causal_item(
                                pair * REP + r, half(e), q_sb[half(e), pair * REP + r, 0:S], 2 * br + pair,
                                lambda kt, br=br, g=g: v_sb[:, kt, br * KV + g * HD:br * KV + (g + 1) * HD],
                                half(e), br == 0, e == 1 and br == 1, (1 + br) * HEADS + h, cmp))
            return items

        def moba_items():
            return [causal_item(h // 2, half(h % 2), q_sb[half(h % 2), h // 2, 0:S], h // 2,
                                lambda kt, h=h: v_sb[:, kt, h * HD:(h + 1) * HD], half(h % 2), True, h % 2 == 1)
                    for h in range(HEADS)]

        def mla_items():
            items = []
            for h in range(MLA_H):
                rows, pt = half(h % 2), h // 2

                def score(qs, ks, h=h, rows=rows, pt=pt):
                    return [(q_sb[:, h, qs], k_sb[:, h, ks]), (pe_sb[rows, pt, qs], pe_sb[rows, 4, ks])]

                def v_of(kt, h=h):
                    return v_sb[:, kt, h * MLA_V:(h + 1) * MLA_V]

                full = slice(0, P)
                none = col("zero")
                items.append(dict(
                    tile=h, last=False, first=True, cols=4 * P, gate=None,
                    scores=[(slice(S * j, S * j + S), score(slice(P * j, P * j + P), CTX)) for j in range(2)],
                    rows=[(slice(S * j, S * j + S), none.to_broadcast([P, S])) for j in range(2)],
                    turns=[(0, 0), (P, 2 * P), (2 * P, P), (3 * P, 3 * P)],
                    pv=[(v_of(kt), slice(S * kt, S * kt + S), CTX, full) for kt in range(2)]))
                for j in range(2):
                    qs = slice(S + P * j, S + P * j + P)
                    items.append(dict(
                        tile=h, last=j == 1, first=True, cols=4 * P, gate=None,
                        scores=[(ALL, score(qs, ALL))], rows=[(ALL, none.to_broadcast([P, 2 * S]))],
                        turns=[(P * i, P * i) for i in range(4)],
                        pv=[(v_of(kt), slice(P * kt, P * kt + P), qs, full) for kt in range(4)]))
            return items

        bias_ring = pe_sb

        def na_items():
            items = []
            for h in range(HEADS):
                for j in range(2):
                    rows, i = half(h % 2), 2 * h + j
                    qs = slice(S + P * j, S + P * j + P)
                    items.append(dict(
                        tile=h // 2, last=h % 2 == 1 and j == 1, first=True, cols=4 * P, gate=None, bias=(h, j),
                        scores=[(ALL, [(q_sb[rows, h // 2, qs], k_sb[rows, h // 2, ALL])])],
                        rows=[(ALL, bias_ring[:, i % 4, :])],
                        turns=[(P * n, P * n) for n in range(4)],
                        pv=[(v_sb[:, kt, h * HD:(h + 1) * HD], slice(P * kt, P * kt + P), slice(P * j, P * j + P), rows)
                            for kt in range(4)]))
            return items

        ITEMS = {"nsa0": nsa_items(), "nsa1": nsa_items(), "moba0": moba_items(), "mla0": mla_items(), "na0": na_items()}
        NEG_SCALE = {"nsa0": -HD ** -0.5, "nsa1": -HD ** -0.5, "moba0": -HD ** -0.5,
                     "mla0": -float(np.float32((NOPE + ROPE) ** -0.5)), "na0": -1.0}
        OUT_COLS = {"nsa0": S, "nsa1": S, "moba0": S, "mla0": 2 * S, "na0": S}
        OUT_TOK = {"nsa0": LAT, "nsa1": LAT, "moba0": LAT, "mla0": ALL, "na0": LAT}

        blk_f = v_sb[:, 2:4, :].rearrange("p a n -> p (a n)")
        NB = 2 * 16 * GROUPS * CS
        blk_hi, blk_lo = hid_hi[:, 0:NB], hid_lo[:, 0:NB]
        kg_hi = hid_hi[:, NB:NB + 2 * GROUPS * CS]
        kg_lo = hid_lo[:, NB:NB + 2 * GROUPS * CS]
        G0 = NB + 2 * GROUPS * CS
        GN = 2 * GROUPS * REP * 32
        vg_hi, vg_lo = hid_hi[:, G0:G0 + GN], hid_lo[:, G0:G0 + GN]
        cmp_s = pe_sb[:, 0, :]
        gel = k_sb[:, 4, 0:4 * GROUPS * CS]
        c_act = [X[:, KD // 2 * j:KD // 2 * (j + 1), CTX] for j in range(2)]
        ada_w = pe_sb[:, 1:5, :].rearrange("p (s a) n -> p s (a n)", s=2)
        p_cmp = k_sb[:, 6:8, :].rearrange("p a n -> p (a n)")
        cq_hi, cq_lo = (h[:, 0:QR * 2 * S].rearrange("p (k t) -> p k t", k=QR) for h in (hid_hi, hid_lo))
        ckv_hi, ckv_lo = (h[:, QR * 2 * S:(QR + KR) * 2 * S].rearrange("p (k t) -> p k t", k=KR) for h in (hid_hi, hid_lo))
        cq_raw = v_sb[:, 0:2, :].rearrange("p a (b t) -> p (a b) t", b=2)
        ckv_raw = v_sb[:, 2, :].rearrange("p (b t) -> p b t", b=2)
        mlp_hi, mlp_lo = (h[:, 0:KD * 2 * S].rearrange("p (k t) -> p k t", k=KD) for h in (hid_hi, hid_lo))
        by_hi, by_lo = (h[:, 0:KD * S].rearrange("p (k t) -> p k t", k=KD) for h in (hid_hi, hid_lo))
        conv_z = v_sb[:, 0:2, :].rearrange("p a (b t) -> p (a b) t", b=4)

        def mods(layer, chunk, k, s):
            j = (layer * ADA_CHUNKS + chunk) * KD + k
            return mod[:, j, s:s + 1]

        block = ctx.enter_context(nc.Block())

        @block.sync
        def _(sp):
            def load(at, i=None, period=0):
                kind, n = STREAM[at]
                n = Num(n, sum(k == kind for k, _ in STREAM[at:at + period]), i)
                if kind == "ada":
                    slot, done = ada_w[:, n.odd, :], ada_landed[n.odd]
                    wait(sp, ada_sum, n.times(2) + 2)
                else:
                    slot, done = stage[:, n.odd, :], landed[n.odd]
                    wait(sp, lo_split, n - 1)
                    wait(sp, lo_rest, n - 1)
                width = STREAM_WIDTHS[at]
                sp.dma_start(slot[:, 0:width], weights[:, bass.ds(Num(at, period, i).times(UC).v, width)]).then_inc(done, 16)

            sp.dma_start(X[:, :, LAT], x_t.rearrange("(k p) t -> p k t", p=P)).then_inc(x_loaded, 16)
            load(0)
            load(1)
            keys = [(kind, n % 2, width) for (kind, n), width in zip(STREAM, STREAM_WIDTHS)]
            at = 2
            while at < len(STREAM):
                period = max((2, 4), key=lambda p: (repeats(keys, at, p) - 1) * p)
                times = repeats(keys, at, period)
                if times > 1:
                    with sp.Fori(0, times) as i:
                        for r in range(period):
                            load(at + r, i, period)
                    at += times * period
                else:
                    load(at)
                    at += 1
            out = out_t.rearrange("(k p) t -> p k t", p=P)
            for h in range(2):
                tiles = slice(h * KD // 2, (h + 1) * KD // 2)
                sp.wait_ge(x_final, tiles.stop)
                sp.dma_start(out[:, tiles, :], X[:, tiles, LAT]).then_inc(stored, 16)
            sp.wait_ge(stored, 32)

        @block.tensor
        def _(pe):
            cnt = Counts()
            n = dict(sq=0, tile=0, hid=0, mean=0, res=0, recip=0, unit=None, fresh=None)

            def mm(out, stationary, moving, start, stop):
                return nc.tensor.matmul(out, stationary, moving, start=start, stop=stop)

            def begin(u):
                wait(pe, lo_split, u + 1)
                n["unit"] = u

            def weights_at(c):
                u = n["unit"]
                if u is not None and c.stop > halves(UNIT_WIDTHS[u.c])[0].stop:
                    wait(pe, lo_rest, u + 1)
                    n["unit"] = None

            def fm_tile(out, slot, tile, x, start, stop):
                c = slice(tile * P, tile * P + P)
                weights_at(c)
                xh, xl = x
                mm(out, w_hi[:, slot, c], xh, start, False)
                mm(out, w_hi[:, slot, c], xl, False, False)
                return mm(out, w_lo[:, slot, c], xh, False, stop)

            def fm(out, slot, tile, xs, start=True, stop=True, tile_at=None):
                for k, x in enumerate(xs):
                    if tile_at:
                        tile_at(k)
                    last = fm_tile(out, slot, tile + k, x, start and k == 0, stop and k == len(xs) - 1)
                return last

            def tm(out, slot, cols, xs):
                for k, (xh, xl) in enumerate(xs):
                    c = cols(k)
                    weights_at(c)
                    mm(out, xh, w_hi[:, slot, c], k == 0, False)
                    mm(out, xl, w_hi[:, slot, c], False, False)
                    last = mm(out, xh, w_lo[:, slot, c], False, k == len(xs) - 1)
                return last

            def start_unit(rings):
                u, made = unit(cnt, rings)
                begin(u)
                return u, made

            def start_product(ring, p):
                wait(pe, taken[ring], p - 1)

            def fm_unit(rings, xs, tile_at=None, each=False):
                u, made = start_unit(rings)
                T = xs[0][0].shape[-1]
                tile_at = tile_at or operand_at
                if (each or n["fresh"] is not None) and len(rings) == 2:
                    for j in range(2):
                        start_product(rings[j], made[j][1])
                    for k, x in enumerate(xs):
                        tile_at(k)
                        for j, (bank, p, (ready, _)) in enumerate(made):
                            last = fm_tile(ps[:, bank, 0:T], u.odd, j * len(xs) + k, x, k == 0, k == len(xs) - 1)
                            if k == len(xs) - 1:
                                last.then_inc(ready, 1)
                    return
                for j, (bank, p, (ready, _)) in enumerate(made):
                    start_product(rings[j], p)
                    fm(ps[:, bank, 0:T], u.odd, j * len(xs), xs, tile_at=None if j else tile_at).then_inc(ready, 1)

            def tm_unit(xs_of, halves, width, ncols):
                u, made = start_unit("D" * len(halves))
                for (bank, p, (ready, _)), (tt, c0) in zip(made, halves):
                    start_product("D", p)
                    tm(ps[:, bank, 0:ncols], u.odd, lambda k: slice(k * width + c0, k * width + c0 + ncols),
                       xs_of(tt)).then_inc(ready, 1)

            def parts(hi, lo, cols=LAT):
                return [(hi[:, k, cols], lo[:, k, cols]) for k in range(hi.shape[1])]

            def sum_squares(nk, T):
                for k in range(nk):
                    pe.wait_ge(sq_ready, n["sq"] + k + 1)
                    mm(ps[:, STAT, 0:T], ones, t_ring[:, (n["sq"] + k) % 2, 0:T], k == 0, k == nk - 1).then_inc(sq_used, 1)
                n["sq"] += nk

            def sum_residual():
                n["res"] += KD
                pe.wait_ge(res_acc, n["res"])
                for j in range(S // P):
                    last = mm(ps[:, STAT, j:j + 1], sq_sum[:, j * P:(j + 1) * P], ones[:, 0:1], True, True)
                last.then_inc(sum_done, 1)
                n["recip"] += 1
                pe.wait_ge(recip_ready, n["recip"])
                for j in range(S // P):
                    last = mm(ps[:, STAT, j * P:(j + 1) * P], stat[:, j:j + 1].to_broadcast([P, P]), ident, True, True)
                last.then_inc(spread_done, 1)

            def operands(nk=KD):
                n["fresh"] = n["tile"]
                n["tile"] += nk

            def operand_at(k):
                if n["fresh"] is not None:
                    pe.wait_ge(operand, n["fresh"] + k + 1)
                    if n["fresh"] + k + 1 == n["tile"]:
                        n["fresh"] = None

            def drained():
                for r in "AD":
                    wait(pe, taken[r], cnt.peek(r))

            def pairs(rings, xs, units):
                fm_unit(rings, xs)
                fm_unit(rings, xs)
                with cnt.loop(pe, units // 2 - 1, unit=2, mid=2, **{r: 2 * rings.count(r) for r in rings}):
                    fm_unit(rings, xs)
                    fm_unit(rings, xs)

            def out_units(src, tile_ready):
                for i in range(4):
                    fm_unit("DD", src, None if i else lambda k: pe.wait_ge(tile_ready, k + 1), i == 0)

            def attention(name, before_turns=None):
                a, items = att[name], ITEMS[name]
                for i in range(len(items) + 3):
                    if i < len(items):
                        it = items[i]
                        if i >= 3:
                            pe.wait_ge(a["s_taken"], i - 2)
                        for c, terms in it["scores"]:
                            for t, (q, k) in enumerate(terms):
                                last = mm(ps[:, S0 + i % 3, c], q, k, t == 0, t == len(terms) - 1)
                        last.then_inc(a["s_ready"], 1)
                    if i == 2 and before_turns:
                        before_turns()
                    if 0 <= i - 2 < len(items):
                        b = i - 2
                        pe.wait_ge(a["p_ready"], b + 1)
                        if b >= 2:
                            pe.wait_ge(a["t_taken"], b - 1)
                        for to, frm in items[b]["turns"]:
                            last = nc.tensor.transpose(ps[:, T0 + b % 2, to:to + P], p_ring[:, b % 3, frm:frm + P], ident)
                        last.then_inc(a["t_ready"], 1)
                    if 0 <= i - 3 < len(items):
                        b = i - 3
                        it = items[b]
                        o = O0 + it["tile"] % 2
                        pe.wait_ge(a["t_taken"], b + 1)
                        if it["tile"] >= 2:
                            pe.wait_ge(a["o_ready"], it["tile"] - 1)
                        for j, (v, t, q, rows) in enumerate(it["pv"]):
                            moving = t_ring[:, b % 2, t] if isinstance(t, slice) else t
                            last = nc.tensor.matmul(ps[rows, o, q], v, moving, start=it["first"] and j == 0,
                                                    stop=j == len(it["pv"]) - 1, skip_group_check=True)
                        last.then_inc(a["pv_done"], 1)

            WIDE = 4 * GROUPS * CS

            def wide(x, i):
                return x[:, i * GROUPS * CS:(i + 1) * GROUPS * CS].unsqueeze(1).to_broadcast([P, 4, GROUPS * CS])

            def run_nsa(j):
                if cnt.n["unit"] == 0:
                    sum_squares(KD, S)
                operands()
                a = parts(a_hi, a_lo)
                for _ in range(2):
                    fm_unit("AA", a)
                for _ in range(4):
                    fm_unit("AA", a)
                for _ in range(2):
                    fm_unit("AA", a)
                for _ in range(2):
                    tm_unit(lambda tt: [(a_hi[:, k, S + tt * P:S + tt * P + P], a_lo[:, k, S + tt * P:S + tt * P + P])
                                        for k in range(KD)], [(0, 0), (1, 0)], KV, KV)
                pe.wait_ge(nsa[j]["blocks_ready"], 1)
                for kv in range(2):
                    for m in range(2):
                        u, [(bank, p, (ready, _))] = start_unit("A")
                        start_product("A", p)
                        N = GROUPS * CS
                        fm(ps[:, bank, 0:WIDE], u.odd, 0, [(wide(blk_hi, kv * 16 + l), wide(blk_lo, kv * 16 + l)) for l in range(16)]
                           ).then_inc(ready, 1)
                u, [(gb, gp, (g_ready, _)), (kb, kp, (k_ready, _)), (vb, vp, (v_ready, _))] = start_unit("AAD")
                start_product("A", gp)
                for tt in range(2):
                    c0 = 2 * P + 2 * HD
                    last = tm(ps[:, gb, tt * 3 * HEADS:(tt + 1) * 3 * HEADS], u.odd,
                              lambda k: slice(c0 + k * 3 * HEADS, c0 + (k + 1) * 3 * HEADS),
                              [(a_hi[:, k, S + tt * P:S + tt * P + P], a_lo[:, k, S + tt * P:S + tt * P + P]) for k in range(KD)])
                last.then_inc(g_ready, 1)
                pe.wait_ge(nsa[j]["gelu_ready"], 2)
                start_product("A", kp)
                N = GROUPS * CS
                fm(ps[:, kb, 0:WIDE], u.odd, 0, [(wide(kg_hi, m), wide(kg_lo, m)) for m in range(2)]
                   ).then_inc(k_ready, 1)
                start_product("D", vp)
                for g in range(GROUPS):
                    last = tm(ps[:, vb, g * HD:(g + 1) * HD], u.odd, lambda m: slice(2 * P + m * HD, 2 * P + (m + 1) * HD),
                              [(vg_hi[:, (m * GROUPS + g) * P:(m * GROUPS + g + 1) * P],
                                vg_lo[:, (m * GROUPS + g) * P:(m * GROUPS + g + 1) * P]) for m in range(2)])
                last.then_inc(v_ready, 1)
                drained()
                for b in range(2):
                    for h in range(HEADS):
                        g, r = divmod(h, REP)
                        rows, t = half(g % 2), g // 2 * REP + r
                        c = (b * HEADS + h) * CS
                        last = mm(ps[:, CMP_BANK[g % 2], c:c + CS], q_sb[rows, t, b * P:(b + 1) * P], k_cmp[rows, g, :], True, True)
                last.then_inc(nsa[j]["cmp_scores"], 1)

                def turn_cmp():
                    pe.wait_ge(nsa[j]["cmp_p"], 1)
                    for g in range(GROUPS):
                        for b in range(2):
                            i = 2 * g + b
                            last = nc.tensor.transpose(ps[:, T0 + i // 4, i % 4 * P:i % 4 * P + P],
                                                       p_cmp[:, (b * HEADS + g * REP) * 32:(b * HEADS + g * REP) * 32 + P], ident)
                    last.then_inc(nsa[j]["cmp_t"], 1)
                    pe.wait_ge(nsa[j]["cmp_t_taken"], 2)

                attention(f"nsa{j}", turn_cmp)
                out_units(parts(a_hi, a_lo), att[f"nsa{j}"]["o_ready"])
                sum_residual()

            def run_moba(_):
                operands()
                a = parts(a_hi, a_lo)
                pairs("AA", a, KD)
                for _ in range(4):
                    tm_unit(lambda tt: [(a_hi[:, k, S + tt * P:S + tt * P + P], a_lo[:, k, S + tt * P:S + tt * P + P])
                                        for k in range(KD)], [(0, 0), (1, 0)], KV, KV)
                drained()
                attention("moba0")
                out_units(parts(a_hi, a_lo), att["moba0"]["o_ready"])
                sum_residual()

            def run_conv(_):
                operands()
                a = parts(a_hi, a_lo)
                pairs("AD", a, KD)
                for _ in range(4):
                    fm_unit("DD", a)
                out_units([(by_hi[:, k, :], by_lo[:, k, :]) for k in range(KD)], conv_ready)
                sum_residual()

            def run_ffn(i):
                operands()
                a = parts(a_hi, a_lo)
                pairs("AD", a, FT)
                n["hid"] += FT
                pe.wait_ge(hid_ready, n["hid"] - FT + HALF_FT)

                def down():
                    u0, _ = unit(cnt, "")
                    begin(u0)
                    u1, [(bank, p, (ready, _))] = unit(cnt, "D")
                    start_product("D", p)
                    for h, u in enumerate((u0, u1)):
                        if h == 1:
                            begin(u1)
                            pe.wait_ge(hid_ready, n["hid"])
                        xs = [(hid_hi[:, f * S:(f + 1) * S], hid_lo[:, f * S:(f + 1) * S])
                              for f in range(h * HALF_FT, (h + 1) * HALF_FT)]
                        fm(ps[:, bank, 0:S], u.odd, 0, xs, h == 0, h == 1).then_inc(unit_done, 1)

                with cnt.loop(pe, 4, unit=4, D=2):
                    down()
                    down()
                sum_residual()

            def layer_mean(T, cols, sem_ready, first):
                for k in range(KD):
                    wait(pe, sem_ready, first + k + 1)
                    last = mm(ps[:, STAT, 0:T], ones, X[:, k, cols], k == 0, k == KD - 1)
                last.then_inc(mean_sum, 1)
                sum_squares(KD, T)

            def run_enter(_):
                pass

            def run_mla(_):
                operands()
                a = parts(a_hi, a_lo, ALL)
                for _ in range(2):
                    fm_unit("AA", a)
                fm_unit("AA", a)
                sum_squares(QR, 2 * S)
                fm_unit("AD", a)
                sum_squares(KR, 2 * S)
                operands(QR)
                cq = parts(cq_hi, cq_lo, ALL)
                for _ in range(2):
                    fm_unit("AAAA", cq)
                fm_unit("AAAA", cq)
                fm_unit("DDDD", cq)
                operands(KR)
                ckv = parts(ckv_hi, ckv_lo, ALL)
                fm_unit("A" * 8, ckv)
                tm_unit(lambda tt: [(ckv_hi[:, k, tt * P:tt * P + P], ckv_lo[:, k, tt * P:tt * P + P]) for k in range(KR)],
                        [(tt, 512 * c) for tt in range(4) for c in range(2)], D, 512)
                drained()
                pe.wait_ge(rope_ready, QR + 1)
                attention("mla0")
                first = cnt.n["D"]
                out_units(parts(a_hi, a_lo, ALL), att["mla0"]["o_ready"])
                layer_mean(2 * S, ALL, taken["D"], first)

            def run_mlp(i):
                cols, T = (ALL, 2 * S) if i == 0 else (LAT, S)
                operands()
                a = parts(a_hi, a_lo, cols)
                hid0 = n["hid"]

                def quarter(q):
                    for _ in range(4):
                        fm_unit("AA", a)
                    for i in range(4):
                        fm_unit("DD", [(mlp_hi[:, k, 0:T], mlp_lo[:, k, 0:T]) for k in range(KD)],
                                None if i else lambda k: wait(pe, hid_ready, q + k + 1))

                with cnt.loop(pe, 4, unit=8, A=8, D=8, mid=8) as i_q:
                    quarter(Num(hid0, KD, i_q))
                n["hid"] += 4 * KD
                layer_mean(T, cols, x_mixed, n["mean"])
                n["mean"] += KD

            def run_na(_):
                operands()
                for _ in range(4):
                    fm_unit("AA", parts(a_hi, a_lo, LAT))
                for _ in range(4):
                    fm_unit("AA", parts(a_hi, a_lo, ALL))
                for _ in range(4):
                    tm_unit(lambda tt: [(a_hi[:, k, tt * P:tt * P + P], a_lo[:, k, tt * P:tt * P + P]) for k in range(KD)],
                            [(tt, 0) for tt in range(4)], KV, KV)
                drained()
                attention("na0")
                first = cnt.n["D"]
                out_units(parts(a_hi, a_lo, LAT), att["na0"]["o_ready"])
                layer_mean(S, LAT, taken["D"], first)

            pe.wait_ge(small_loaded, 16)
            run = dict(nsa=run_nsa, ffn=run_ffn, moba=run_moba, conv=run_conv, enter=run_enter, mla=run_mla, mlp=run_mlp, na=run_na)
            for stage_name, arg in PROGRAM:
                run[stage_name](arg)

        @block.scalar
        def _(act):
            cnt = Counts()
            n = dict(sq=0, std=0, sum=0, tile=0, mean=0, centered=0, step=0, later=lambda: None)

            def step(ins):
                ins.then_inc(act_step, 1)
                n["step"] += 1

            def split(u):
                if not isinstance(u, Num):
                    u = Num(u)
                width = UNIT_WIDTHS[u.c]
                wait(act, landed[u.odd], (u.half + 1).times(16))
                wait(act, unit_done, u - 1)
                for c in halves(width):
                    nc.scalar.copy(w_hi[:, u.odd, c], stage[:, u.odd, c]).then_inc(hi_split, 1)

            def ahead(u):
                if u.reg is not None or u.c + 2 < U:
                    split(u + 2)

            def later():
                n["later"]()
                n["later"] = lambda: None

            def next_unit(rings):
                return unit(cnt, rings)

            def drain(dst, made, rows=slice(0, P), func=None, **kw):
                bank, p, (ready, count) = made
                wait(act, ready, count)
                src = ps[rows, bank, 0:dst.free_size()]
                if len(dst.shape) == 3:
                    src = src.rearrange("p (a b) -> p a b", a=dst.shape[1])
                nc.scalar.activation(dst, src, func or ACT.Copy, **kw).then_inc(taken["A"], 1)

            def squares(nk, src, T, ready):
                for k in range(nk):
                    s_, c = ready(k)
                    wait(act, s_, c)
                    wait(act, sq_used, n["sq"] + k - 1)
                    nc.scalar.activation(t_ring[:, (n["sq"] + k) % 2, 0:T], src(k), ACT.Square).then_inc(sq_ready, 1)
                n["sq"] += nk

            def deviation(T, dim, eps):
                act.wait_ge(sq_used, n["sq"])
                nc.scalar.activation(rstd[:, 0:T], ps[:, STAT, 0:T], ACT.Sqrt, bias=col(eps), scale=1.0 / dim
                                     ).then_inc(std_ready, 1)

            def high_tiles(nk, dst, T):
                for k in range(nk):
                    act.wait_ge(normed, n["tile"] + k + 1)
                    nc.scalar.copy(dst(k), p_ring[:, k % 2, 0:T]).then_inc(norm_hi, 1)
                n["tile"] += nk

            def residual_square(made, x):
                r = cnt.next("res")
                wait(act, taken["D"], made[1] + 1)
                wait(act, res_acc, r - 1)
                nc.scalar.activation(t_ring[:, r.odd, 0:S], x, ACT.Square).then_inc(res_sq, 1)

            def ready_sqrt():
                act.wait_ge(act_step, n["step"])
                step(nc.scalar.activation(spare[:, :], col("ones", 0, 1), ACT.Sqrt))

            def residual_deviation():
                n["sum"] += 1
                act.wait_ge(sum_done, n["sum"])
                nc.scalar.activation(stat[:, 0:S // P], ps[:, STAT, 0:S // P], ACT.Sqrt, bias=col("rms_eps"), scale=1.0 / D
                                     ).then_inc(std_ready, 1)

            def mixer_ends():
                for i in range(4):
                    u, made = next_unit("DD")
                    if i == 3:
                        ready_sqrt()
                    for m in range(2):
                        residual_square(made[m], X[:, 2 * i + m, LAT])
                    if i < 3:
                        ahead(u)
                residual_deviation()
                n["later"] = lambda: ahead(u)

            def rms_operand():
                if cnt.n["unit"] == 0:
                    ready_sqrt()
                    squares(KD // 2, lambda k: X[:, k, LAT], S, lambda k: (x_loaded, 16))
                    split(0)
                    squares(KD // 2, lambda k: X[:, KD // 2 + k, LAT], S, lambda k: (x_loaded, 16))
                    deviation(S, D, "rms_eps")
                    n["later"] = lambda: split(1)
                    for j in range(2):
                        act.dma_start(c_act[j], c_rows[:, j].rearrange("p (a b) -> p a b", b=S)).then_inc(c_loaded, 16)
                high_tiles(KD, lambda k: a_hi[:, k, LAT], S)
                later()

            def layer_norm(cols, T, last=False, next_T=None, next_cols=None):
                n["mean"] += 1
                ready_sqrt()
                act.wait_ge(mean_sum, n["mean"])
                nc.scalar.activation(rstd[:, 0:T], ps[:, STAT, 0:T], ACT.Copy, scale=1.0 / D).then_inc(mean_ready, 1)
                c0 = n["centered"]
                squares(KD, lambda k: X[:, k, cols], T, lambda k: (centered, c0 + k + 1))
                n["centered"] += KD
                deviation(T, D, "ln_eps")
                if not last:
                    high_tiles(KD, lambda k: a_hi[:, k, next_cols], next_T)
                later()

            def attention(name, load_bias=None):
                a, items = att[name], ITEMS[name]
                for i in range(len(items) + 3):
                    if i < len(items):
                        act.wait_ge(a["s_taken"], i + 1)
                        for r, (c, _) in enumerate(items[i]["rows"]):
                            last = nc.scalar.activation(p_ring[:, i % 3, c], p_ring[:, i % 3, c], ACT.Exp,
                                                        bias=negmax[:, i % 4, r:r + 1], scale=-1.0,
                                                        accum_out=sums[:, i % 4, r:r + 1])
                        last.then_inc(a["exp_done"], 1)
                        if load_bias and i + 4 < len(items):
                            load_bias(i + 4)
                    b = i - 1
                    if 0 <= b < len(items):
                        act.wait_ge(a["t_ready"], b + 1)
                        if b >= 2:
                            act.wait_ge(a["pv_done"], b - 1)
                        c = items[b]["cols"]
                        nc.scalar.copy(t_ring[:, b % 2, 0:c], ps[:, T0 + b % 2, 0:c]).then_inc(a["t_taken"], 1)
                    b = i - 3
                    if 0 <= b and items[b]["last"]:
                        act.wait_ge(a["pv_done"], b + 1)
                        t = items[b]["tile"]
                        nc.scalar.copy(a_hi[:, t, OUT_TOK[name]], ps[:, O0 + t % 2, 0:OUT_COLS[name]]).then_inc(a["o_hi"], 1)

            def skip(rings, times=1):
                for _ in range(times):
                    u, _ = next_unit(rings)
                    ahead(u)

            def run_nsa(j):
                rms_operand()
                s = nsa[j]
                for kv in range(2):
                    u, made = next_unit("AA")
                    for pair in range(2):
                        drain(k_sb[:, 4 + kv, pair * S:(pair + 1) * S], made[pair])
                    ahead(u)
                act.wait_ge(taken["A"], cnt.n["A"])
                q_spare = q_sb[:, :, S:2 * S].rearrange("p (a e) t -> p a e t", e=2)
                for e in range(2):
                    for to in range(2):
                        act.dma_start(q_spare[half(to), :, e, :],
                                      k_sb[half(e), 4:6, :].rearrange("p a (b t) -> p (a b) t", b=2)).then_inc(s["shifted"], 16)
                for i in range(4):
                    u, made = next_unit("AA")
                    for m in range(2):
                        drain(q_sb[:, 2 * i + m, 0:S], made[m])
                    ahead(u)
                for br in range(2):
                    u, made = next_unit("AA")
                    for pair in range(2):
                        drain(k_sb[:, 2 * br + pair, 0:S], made[pair])
                    ahead(u)
                act.wait_ge(s["blocks"], 8)
                nc.scalar.copy(blk_hi, blk_f).then_inc(s["blocks_hi"], 1)
                skip("DD", 2)
                for i in range(4):
                    u, made = next_unit("A")
                    drain(gel[:, i * GROUPS * CS:(i + 1) * GROUPS * CS], made[0], func=ACT.Gelu_apprx_tanh)
                    ahead(u)
                u, made = next_unit("AAD")
                drain(gate[:, :, :], made[0], func=ACT.Sigmoid)
                drain(k_cmp[:, :, :], made[1])
                ahead(u)
                act.wait_ge(s["cmp_shifted"], 1)
                nc.scalar.activation(cmp_s, cmp_s, ACT.Exp, scale=HD ** -0.5).then_inc(s["cmp_exp"], 1)
                act.wait_ge(s["cmp_t"], 1)
                for b in range(2):
                    nc.scalar.copy(v_sb[:, 2, b * 512:(b + 1) * 512], ps[:, T0 + b, :]).then_inc(s["cmp_t_taken"], 1)
                attention(f"nsa{j}")
                if j == 0:
                    act.wait_ge(c_loaded, 32)
                    for c in c_act:
                        ins = nc.scalar.activation(c, c, ACT.Silu)
                        ins.then_inc(ada_sum, 2)
                mixer_ends()

            def run_moba(_):
                rms_operand()
                t0 = cnt.n["A"]
                with cnt.loop(act, 4, unit=2, A=4, mid=2):
                    for _ in range(2):
                        u, made = next_unit("AA")
                        for m in range(2):
                            t = made[m][1] - t0
                            drain(qk[:, bass.ds(t.v, 1), 0:S].rearrange("p a t -> p (a t)"), made[m])
                        ahead(u)
                skip("DD", 4)
                attention("moba0")
                mixer_ends()

            def run_conv(_):
                rms_operand()

                def pair():
                    u, made = next_unit("AD")
                    p = made[0][1]
                    wait(act, taken["D"], made[1][1] - 1)
                    drain(p_ring[:, p.odd, 0:S], made[0])
                    ahead(u)

                with cnt.loop(act, 4, unit=2, A=2, D=2, mid=2):
                    pair()
                    pair()
                skip("DD", 4)
                mixer_ends()

            def run_ffn(i):
                rms_operand()
                h0 = cnt.n["hid"]

                def gate_up():
                    u, made = next_unit("AD")
                    h = cnt.next("hid")
                    wait(act, taken["D"], made[1][1] - 1)
                    drain(p_ring[:, made[0][1].odd, 0:S], made[0], func=ACT.Silu)
                    ahead(u)
                    wait(act, taken["D"], made[1][1] + 1)
                    nc.scalar.copy(hid_hi[:, bass.ds((h - h0).times(S).v, S)], t_ring[:, h.odd, 0:S]).then_inc(hid_h, 1)

                with cnt.loop(act, FT // 2 - 1, unit=2, A=2, D=2, mid=2, hid=2):
                    gate_up()
                    gate_up()
                gate_up()
                gate_up()
                d0 = cnt.n["D"]

                def down():
                    skip("")
                    u, [made] = next_unit("D")
                    residual_square(made, X[:, bass.ds((made[1] - d0).v, 1), LAT].rearrange("p a t -> p (a t)"))
                    return u

                with cnt.loop(act, 3, unit=4, D=2, res=2):
                    ahead(down())
                    ahead(down())
                if i == 3:
                    act.wait_ge(ada_sum, 2 * ADA_UNITS + 4)
                    act.dma_start(X[:, :, CTX], ctx_t.rearrange("(k p) t -> p k t", p=P)).then_inc(ctx_loaded, 16)
                ahead(down())
                ready_sqrt()
                u = down()
                residual_deviation()
                n["later"] = lambda: ahead(u)

            def run_enter(_):
                if PROGRAM[-1][0] != "enter":
                    high_tiles(KD, lambda k: a_hi[:, k, ALL], 2 * S)
                    later()

            def run_mla(_):
                a0 = cnt.n["A"]
                for i in range(3):
                    u, made = next_unit("AA")
                    for m in range(2):
                        drain(cq_raw[:, 2 * i + m, :] if i < 2 else ckv_raw[:, m, :], made[m])
                    ahead(u)
                squares(QR, lambda k: cq_raw[:, k, :], 2 * S, lambda k: (taken["A"], a0 + k + 1))
                deviation(2 * S, Q_RANK, "rms_eps")
                high_tiles(QR, lambda k: cq_hi[:, k, :], 2 * S)
                u, made = next_unit("AD")
                drain(pe_sb[:, 4, :], made[0])
                ahead(u)
                squares(KR, lambda k: ckv_raw[:, k, :], 2 * S, lambda k: (taken["A"], a0 + QR + k + 1))
                deviation(2 * S, KV_RANK, "rms_eps")
                high_tiles(KR, lambda k: ckv_hi[:, k, :], 2 * S)
                for i in range(3):
                    u, made = next_unit("AAAA")
                    for m in range(4):
                        drain(q_sb[:, 4 * i + m, :] if i < 2 else pe_sb[:, m, :], made[m])
                    ahead(u)
                skip("DDDD")
                u, made = next_unit("A" * 8)
                for h in range(MLA_H):
                    drain(k_sb[:, h, :], made[h])
                ahead(u)
                skip("D" * 8)
                attention("mla0")
                skip("DD", 4)
                layer_norm(ALL, 2 * S, next_T=2 * S, next_cols=ALL)

            def run_mlp(i):
                cols, T = (ALL, 2 * S) if i == 0 else (LAT, S)

                def quarter():
                    for _ in range(4):
                        u, made = next_unit("AA")
                        for m in range(2):
                            wait(act, hid_f, cnt.next("relu") - 1)
                            drain(p_ring[:, made[m][1].odd, 0:T], made[m], func=ACT.Relu)
                        ahead(u)
                    skip("DD", 4)

                with cnt.loop(act, 3, unit=8, A=8, D=8, mid=8, relu=8):
                    quarter()
                quarter()
                layer_norm(cols, T, last=i == 1, next_T=2 * S, next_cols=ALL)

            def run_na(_):
                scaled = sm[:, SMALL["na_bq"]]
                step(nc.scalar.mul(scaled, scaled, HD ** -0.5))
                act.wait_ge(operand, n["tile"])
                act.dma_start(p_ring[:, 0:2, :].rearrange("p a b -> p (a b)"), na_bv).then_inc(bv_loaded, 16)
                act.wait_ge(act_step, n["step"])
                for i in range(4):
                    u, made = next_unit("AA")
                    for m in range(2):
                        drain(q_sb[:, 2 * i + m, LAT], made[m], func=ACT.Identity, scale=HD ** -0.5, bias=col("na_bq", 2 * i + m))
                    ahead(u)
                for i in range(4):
                    u, made = next_unit("AA")
                    for m in range(2):
                        drain(k_sb[:, 2 * i + m, :], made[m], func=ACT.Identity, bias=col("na_bk", 2 * i + m))
                    ahead(u)

                def load_bias(i):
                    h, j = ITEMS["na0"][i]["bias"]
                    act.dma_start(bias_ring[:, i % 4, S:2 * S], na_bias[h, j]).then_inc(bias_loaded[i % 4], 16)

                for i in range(4):
                    load_bias(i)
                skip("DDDD", 4)
                attention("na0", load_bias)
                skip("DD", 4)
                layer_norm(LAT, S, next_T=S, next_cols=LAT)

            act.dma_start(sm[:, :], small).then_inc(small_loaded, 16)
            act.wait_ge(small_loaded, 16)
            run = dict(nsa=run_nsa, ffn=run_ffn, moba=run_moba, conv=run_conv, enter=run_enter, mla=run_mla, mlp=run_mlp, na=run_na)
            for stage_name, arg in PROGRAM:
                run[stage_name](arg)

        @block.vector
        def _(dve):
            cnt = Counts()
            n = dict(std=0, spread=0, tile=0, mean=0, step=0, norm=0, last=False, later=lambda: None)
            v = nc.vector

            def step(ins):
                ins.then_inc(dve_step, 1)
                n["step"] += 1

            def sync():
                dve.wait_ge(dve_step, n["step"])

            def minus(out, a, b):
                return v.tensor_tensor(out, a, b.bitcast(F32), ALU.subtract)

            def split(u):
                if not isinstance(u, Num):
                    u = Num(u)
                width = UNIT_WIDTHS[u.c]
                c = halves(width)[0]
                wait(dve, hi_split, u.times(2) + 1)
                minus(w_lo[:, u.odd, c], stage[:, u.odd, c], w_hi[:, u.odd, c]).then_inc(lo_split, 1)

            def ahead(u):
                if u.reg is not None or u.c + 2 < U:
                    split(u + 2)

            def later():
                n["later"]()
                n["later"] = lambda: None

            def next_unit(rings):
                return unit(cnt, rings)

            def skip(rings, times=1):
                for _ in range(times):
                    u, _ = next_unit(rings)
                    ahead(u)

            def ready(made):
                bank, p, (s_, c) = made
                wait(dve, s_, c)
                return bank

            def ada_tile():
                a = cnt.next("ada")
                wait(dve, ada_landed[a.odd], (a.half + 1).times(16))
                for s_ in range(2):
                    wait(dve, ada_sum, a.times(2) + (4 + s_))
                    v.tensor_tensor_reduce(products, ada_w[:, a.odd, :].rearrange("p (a b) -> p a b", b=S), c_act[s_], 1.0, 0.0,
                                           ALU.mult, ALU.add, mod_sum[:, a.odd, s_:s_ + 1]).then_inc(ada_sum, 1)
                wait(dve, ada_sum, a.times(2) + 6)
                v.tensor_copy(mod[:, bass.ds(a.v, 1), :], mod_sum[:, a.odd:a.odd + 1, :]).then_inc(mod_ready, 1)
                wait(dve, mod_ready, a + 1)

            def reciprocal_deviation(T):
                n["std"] += 1
                dve.wait_ge(std_ready, n["std"])
                step(v.reciprocal(rstd[:, 0:T], rstd[:, 0:T]))
                sync()

            def residual_deviation():
                n["std"] += 1
                dve.wait_ge(std_ready, n["std"])
                v.reciprocal(stat[:, :], stat[:, :]).then_inc(recip_ready, 1)
                n["spread"] += 1
                dve.wait_ge(spread_done, n["spread"])

            def operand_tiles(nk, make, hi, lo, T):
                for k in range(nk + 1):
                    if k < nk:
                        wait(dve, operand, n["tile"] + max(k - 1, 0))
                        make(k, p_ring[:, k % 2, 0:T]).then_inc(normed, 1)
                    if k >= 1:
                        dve.wait_ge(norm_hi, n["tile"] + k)
                        minus(lo(k - 1), p_ring[:, (k - 1) % 2, 0:T], hi(k - 1)).then_inc(operand, 1)
                n["tile"] += nk

            def rms_operand(gain):
                r = ps[:, STAT, 0:S]
                if cnt.n["unit"] == 0:
                    split(0)
                    reciprocal_deviation(S)
                    r = rstd[:, 0:S]
                    n["later"] = lambda: split(1)
                operand_tiles(KD, lambda k, t: v.scalar_tensor_tensor(t, X[:, k, LAT], gain(k), r, ALU.mult, ALU.mult),
                              lambda k: a_hi[:, k, LAT], lambda k: a_lo[:, k, LAT], S)
                later()

            HALVES = [(CTX, 1), (LAT, 0)]

            def modulate(layer, chunk, cols):
                parts = HALVES if cols == ALL else [(LAT, 0)]
                T = S * len(parts)

                def make(k, t):
                    for i, (c, s_) in enumerate(parts):
                        last = v.tensor_scalar(t[:, i * S:(i + 1) * S], X[:, k, c], mods(layer, chunk + 1, k, s_),
                                               mods(layer, chunk, k, s_), ALU.mult, ALU.add)
                    return last

                operand_tiles(KD, make, lambda k: a_hi[:, k, cols], lambda k: a_lo[:, k, cols], T)

            def layer_norm(cols, T, gname, bname, layer, then=None):
                g, b = col(gname, layer * KD, KD), col(bname, layer * KD, KD)
                if then:
                    next_layer, chunk, op_cols, res_cols = then
                    j = (next_layer * ADA_CHUNKS + chunk) * KD
                    shift, scale = mod[:, j:j + KD, :], mod[:, j + KD:j + 2 * KD, :]
                    step(v.tensor_tensor(mod_g[:, :, :], scale, g.unsqueeze(2).to_broadcast([P, KD, 2]), ALU.mult))
                    step(v.tensor_tensor(mod_b[:, :, :], scale, b.unsqueeze(2).to_broadcast([P, KD, 2]), ALU.mult))
                    step(v.tensor_scalar(alpha_g[:, :], g, ALPHA, None, ALU.mult))
                    step(v.tensor_scalar(alpha_b[:, :], b, ALPHA, None, ALU.mult))
                    sync()
                    step(v.tensor_tensor(mod_b[:, :, :], mod_b[:, :, :], shift, ALU.add))
                    sync()
                n["mean"] += 1
                dve.wait_ge(mean_ready, n["mean"])
                for k in range(KD):
                    v.tensor_tensor(X[:, k, cols], X[:, k, cols], rstd[:, 0:T], ALU.subtract).then_inc(centered, 1)
                reciprocal_deviation(T)
                if not then:
                    for half_ in range(2):
                        tiles = range(half_ * KD // 2, (half_ + 1) * KD // 2)
                        for k in tiles:
                            step(v.tensor_tensor(X[:, k, cols], X[:, k, cols], rstd[:, 0:T], ALU.mult))
                        sync()
                        for k in tiles:
                            v.tensor_scalar(X[:, k, cols], X[:, k, cols], g[:, k:k + 1], b[:, k:k + 1], ALU.mult, ALU.add
                                            ).then_inc(x_final, 1)
                    return
                parts = HALVES if op_cols == ALL else [(LAT, 0)]

                def make(k, t):
                    v.tensor_tensor(X[:, k, cols], X[:, k, cols], rstd[:, 0:T], ALU.mult).then_inc(x_norm, 1)
                    n["norm"] += 1
                    dve.wait_ge(x_norm, n["norm"])
                    for i, (c, s_) in enumerate(parts):
                        last = v.tensor_scalar(t[:, i * S:(i + 1) * S], X[:, k, c], mod_g[:, k, s_:s_ + 1], mod_b[:, k, s_:s_ + 1],
                                               ALU.mult, ALU.add)
                    return last

                operand_tiles(KD, make, lambda k: a_hi[:, k, op_cols], lambda k: a_lo[:, k, op_cols], S * len(parts))
                for k in range(KD):
                    step(v.tensor_scalar(X[:, k, res_cols], X[:, k, res_cols], alpha_g[:, k:k + 1], alpha_b[:, k:k + 1],
                                         ALU.mult, ALU.add))

            def scale_residual(cols):
                for k in range(KD):
                    step(v.tensor_scalar(X[:, k, cols], X[:, k, cols], ALPHA, None, ALU.mult))

            def add_square():
                r = cnt.next("res")
                wait(dve, res_sq, r + 1)
                wait(dve, res_acc, r)
                v.tensor_tensor(sq_sum, sq_sum, t_ring[:, r.odd, 0:S], ALU.add).then_inc(res_acc, 1)

            def mixer_ends():
                step(v.memset(sq_sum, 0.0))
                sync()
                for i in range(4):
                    u, made = next_unit("DD")
                    for m in range(2):
                        bank = ready(made[m])
                        k = 2 * i + m
                        v.tensor_tensor(X[:, k, LAT], ps[:, bank, 0:S], X[:, k, LAT], ALU.add).then_inc(taken["D"], 1)
                    for m in range(2):
                        add_square()
                    if i < 3:
                        ahead(u)
                residual_deviation()
                n["later"] = lambda: ahead(u)

            def gated_residual_units(layer, chunk, cols):
                sync()
                for i in range(4):
                    u, made = next_unit("DD")
                    for m in range(2):
                        bank = ready(made[m])
                        k = 2 * i + m
                        for c, s_ in HALVES if cols == ALL else [(LAT, 0)]:
                            src = ps[:, bank, c] if cols == ALL else ps[:, bank, 0:S]
                            last = v.scalar_tensor_tensor(X[:, k, c], src, mods(layer, chunk, k, s_), X[:, k, c],
                                                          ALU.mult, ALU.add)
                        last.then_inc(taken["D"], 1)
                    ahead(u)

            def attention(name, bias=False):
                a, items = att[name], ITEMS[name]
                tiles = 0
                for i in range(len(items) + 4):
                    if i < len(items):
                        dve.wait_ge(a["s_ready"], i + 1)
                        if i >= 3:
                            dve.wait_ge(a["t_ready"], i - 2)
                        if bias:
                            dve.wait_ge(bias_loaded[i % 4], 16 * (i // 4 + 1))
                        for r, (c, mask) in enumerate(items[i]["rows"]):
                            last = v.tensor_tensor_reduce(p_ring[:, i % 3, c], ps[:, S0 + i % 3, c], mask, NEG_SCALE[name], 3e38,
                                                          ALU.add, ALU.min, negmax[:, i % 4, r:r + 1])
                        last.then_inc(a["s_taken"], 1)
                    b = i - 1
                    if 0 <= b < len(items):
                        w = len(items[b]["rows"])
                        g = items[b]["gate"]
                        dve.wait_ge(a["exp_done"], b + 1)
                        step(v.reciprocal(recip[:, b % 4, 0:w], sums[:, b % 4, 0:w]))
                        if g is not None:
                            sync()
                            step(v.tensor_tensor(recip[:, b % 4, 0:w], recip[:, b % 4, 0:w], gate[:, :, g], ALU.mult))
                        sync()
                        for r, (c, _) in enumerate(items[b]["rows"]):
                            last = v.tensor_scalar(p_ring[:, b % 3, c], p_ring[:, b % 3, c], recip[:, b % 4, r:r + 1], None, ALU.mult)
                        last.then_inc(a["p_ready"], 1)
                    b = i - 4
                    if 0 <= b and items[b]["last"]:
                        tiles += 1
                        dve.wait_ge(a["o_hi"], tiles)
                        t = items[b]["tile"]
                        minus(a_lo[:, t, OUT_TOK[name]], ps[:, O0 + t % 2, 0:OUT_COLS[name]], a_hi[:, t, OUT_TOK[name]]
                              ).then_inc(a["o_ready"], 1)

            def values(rings, unit_col, width, add=None):
                u, made = next_unit(rings)
                for tt, m in enumerate(made):
                    bank = ready(m)
                    dst = v_sb[:, tt, unit_col:unit_col + width]
                    if add is None:
                        ins = v.tensor_copy(dst, ps[:, bank, 0:width])
                    else:
                        ins = v.tensor_tensor(dst, ps[:, bank, 0:width], add, ALU.add)
                    ins.then_inc(taken["D"], 1)
                ahead(u)

            def run_nsa(j):
                rms_operand(lambda k: col("norm_mix", 3 * j * KD + k))
                s = nsa[j]
                skip("AA", 4)
                v_rep = [h.rearrange("p (m g r c) -> p m g r c", m=2, g=GROUPS, r=REP) for h in (vg_hi, vg_lo)]
                step(v.memset(vg_hi.bitcast(F32), 0.0))
                step(v.memset(vg_lo.bitcast(F32), 0.0))
                step(v.memset(p_cmp, 0.0))
                blocks = blk_f.rearrange("p (kv l g c) -> p kv l g c", kv=2, l=16, g=GROUPS)
                step(v.memset(blk_f.rearrange("p (n c) -> p n c", c=CS)[:, :, N_CMP:CS], 0.0))
                dve.wait_ge(s["shifted"], 64)
                for kv in range(2):
                    for par in range(2):
                        src = q_sb[half(par), kv * GROUPS:(kv + 1) * GROUPS, S:2 * S].rearrange("p g (c o) -> p g c o", o=CMP_STRIDE)
                        pos = sm[half(par), SMALL["pos"].start + (j * 2 + kv) * 16:SMALL["pos"].start + (j * 2 + kv) * 16 + 16]
                        for late in range(2):
                            for g in range(GROUPS):
                                at = src[:, g, late:late + N_CMP, par:CMP_STRIDE:2].rearrange("p c l -> p l c")
                                ps_ = pos[:, late * 8:late * 8 + 8].unsqueeze(2).to_broadcast([HD, 8, N_CMP])
                                ins = v.tensor_tensor(blocks[half(par), kv, late * 8:late * 8 + 8, g, 0:N_CMP], at, ps_, ALU.add)
                            ins.then_inc(s["blocks"], 1)
                skip("AA", 4)
                dve.wait_ge(s["blocks_hi"], 1)
                sync()
                minus(blk_lo, blk_f, blk_hi).then_inc(s["blocks_ready"], 1)
                for br in range(2):
                    values("DD", br * KV, KV)
                a0 = cnt.n["A"]
                skip("A", 4)
                u, made = next_unit("AAD")
                N = GROUPS * CS
                dve.wait_ge(taken["A"], a0 + 2)
                step(v.tensor_copy(kg_hi, gel[:, 0:2 * N]))
                sync()
                minus(kg_lo, gel[:, 0:2 * N], kg_hi).then_inc(s["gelu_ready"], 1)
                dve.wait_ge(taken["A"], a0 + 4)
                rep = [gel[:, (2 + m) * N:(3 + m) * N].rearrange("p (g c) -> p g c", g=GROUPS).unsqueeze(2)
                       .to_broadcast([P, GROUPS, REP, CS]) for m in range(2)]
                for m in range(2):
                    step(v.tensor_copy(v_rep[0][:, m, :, :, 0:CS], rep[m]))
                sync()
                for m in range(2):
                    ins = minus(v_rep[1][:, m, :, :, 0:CS], rep[m], v_rep[0][:, m, :, :, 0:CS])
                ins.then_inc(s["gelu_ready"], 1)
                v_blk = v_sb[:, 3, :].rearrange("p (g r d) -> p g r d", g=GROUPS, r=REP)
                dve.wait_ge(s["blocks_ready"], 1)
                step(v.memset(v_sb[:, 3, :], 0.0))
                bank = ready(made[2])
                sync()
                for r in range(REP):
                    rows = slice(32 * r, 32 * r + 32)
                    ins = v.tensor_copy(v_blk[rows, :, r, :], ps[rows, bank, 0:KV].rearrange("p (g d) -> p g d", g=GROUPS))
                ins.then_inc(taken["D"], 1)
                ahead(u)
                dve.wait_ge(s["cmp_scores"], 1)
                rows3 = cmp_s.rearrange("p (n c) -> p n c", c=CS)
                for b in range(2):
                    mask = sm[:, SMALL["cmp_mask"].start + b * CS:SMALL["cmp_mask"].start + (b + 1) * CS]
                    mask = mask.unsqueeze(1).unsqueeze(1).to_broadcast([P, 2, REP, CS])
                    for e in range(2):
                        shape = dict(pair=2, e=2, r=REP)
                        to = cmp_s[:, b * S:(b + 1) * S].rearrange("p (pair e r c) -> p pair e r c", **shape)[:, :, e]
                        of = ps[:, CMP_BANK[e], b * S:(b + 1) * S].rearrange("p (pair e r c) -> p pair e r c", **shape)[:, :, e]
                        step(v.tensor_tensor(to, of, mask, ALU.add))
                sync()
                step(v.tensor_reduce(cmp_max[:, :], rows3, AX_X, ALU.max))
                sync()
                v.tensor_tensor(rows3, rows3, cmp_max[:, :].unsqueeze(2).to_broadcast([P, 2 * HEADS, CS]), ALU.subtract
                                ).then_inc(s["cmp_shifted"], 1)
                dve.wait_ge(s["cmp_exp"], 1)
                step(v.tensor_reduce(cmp_sum[:, :], rows3, AX_X, ALU.add))
                sync()
                step(v.reciprocal(cmp_sum[:, :], cmp_sum[:, :]))
                sync()
                for b in range(2):
                    c = slice(b * HEADS, (b + 1) * HEADS)
                    step(v.scalar_tensor_tensor(cmp_sum[:, c], cmp_sum[:, c], col("valid", b), gate[:, b, 0:HEADS],
                                                ALU.mult, ALU.mult))
                sync()
                v.tensor_tensor(p_cmp.rearrange("p (n c) -> p n c", c=32)[:, :, 0:CS], rows3,
                                cmp_sum[:, :].unsqueeze(2).to_broadcast([P, 2 * HEADS, CS]), ALU.mult).then_inc(s["cmp_p"], 1)
                attention(f"nsa{j}")
                mixer_ends()

            def run_moba(_):
                rms_operand(lambda k: col("norm_mix", KD + k))
                with cnt.loop(dve, 4, unit=2, A=4, mid=2):
                    skip("AA", 2)
                for i in range(4):
                    values("DD", i * KV, KV)
                attention("moba0")
                mixer_ends()

            def run_conv(_):
                rms_operand(lambda k: col("norm_mix", 2 * KD + k))
                d0 = cnt.n["D"]

                def product():
                    u, made = next_unit("AD")
                    bank = ready(made[1])
                    wait(dve, taken["A"], made[0][1] + 1)
                    f = made[1][1] - d0
                    v.tensor_tensor(conv_z[:, bass.ds(f.v, 1), :].rearrange("p a t -> p (a t)"), ps[:, bank, 0:S],
                                    p_ring[:, made[0][1].odd, 0:S], ALU.mult).then_inc(taken["D"], 1)
                    ahead(u)

                with cnt.loop(dve, 4, unit=2, A=2, D=2, mid=2):
                    product()
                    product()
                dve.wait_ge(taken["D"], cnt.n["D"])
                for i in range(4):
                    u, made = next_unit("DD")
                    for m in range(2):
                        k = 2 * i + m
                        y = t_ring[:, k % 2, 0:S]
                        wait(dve, conv_ready, k - 1)
                        w = [col("conv_w", j * KD + k) for j in range(3)]
                        z = conv_z[:, k, :]
                        step(v.tensor_scalar(y, z, w[2], None, ALU.mult))
                        sync()
                        step(v.scalar_tensor_tensor(y[:, 1:S], z[:, 0:S - 1], w[1], y[:, 1:S], ALU.mult, ALU.add))
                        sync()
                        step(v.scalar_tensor_tensor(y[:, 2:S], z[:, 0:S - 2], w[0], y[:, 2:S], ALU.mult, ALU.add))
                        sync()
                        bank = ready(made[m])
                        v.tensor_tensor(y, ps[:, bank, 0:S], y, ALU.mult).then_inc(taken["D"], 1)
                        dve.wait_ge(taken["D"], made[m][1].c + 1)
                        v.tensor_copy(by_hi[:, k, :], y).then_inc(conv_hi, 1)
                        dve.wait_ge(conv_hi, k + 1)
                        minus(by_lo[:, k, :], y, by_hi[:, k, :]).then_inc(conv_ready, 1)
                    ahead(u)
                mixer_ends()

            def run_ffn(i):
                rms_operand(lambda k: col("norm_ffn", i * KD + k))
                h0 = cnt.n["hid"]

                def gate_up():
                    u, made = next_unit("AD")
                    h = cnt.next("hid")
                    wait(dve, taken["A"], made[0][1] + 1)
                    bank = ready(made[1])
                    y = t_ring[:, h.odd, 0:S]
                    v.tensor_tensor(y, ps[:, bank, 0:S], p_ring[:, made[0][1].odd, 0:S], ALU.mult).then_inc(taken["D"], 1)
                    c = bass.ds((h - h0).times(S).v, S)
                    ahead(u)
                    wait(dve, hid_h, h + 1)
                    minus(hid_lo[:, c], y, hid_hi[:, c]).then_inc(hid_ready, 1)
                    wait(dve, hid_ready, h + 1)

                with cnt.loop(dve, FT // 2 - 1, unit=2, ada=2, A=2, D=2, mid=2, hid=2):
                    for _ in range(2):
                        gate_up()
                        ada_tile()
                gate_up()
                gate_up()
                d0 = cnt.n["D"]

                step(v.memset(sq_sum, 0.0))
                sync()

                def down(last=False):
                    u0, _ = next_unit("")
                    if not last:
                        ahead(u0)
                    u1, [made] = next_unit("D")
                    bank = ready(made)
                    x = X[:, (made[1] - d0).c, LAT]
                    v.tensor_tensor(x, ps[:, bank, 0:S], x, ALU.add).then_inc(taken["D"], 1)
                    if last:
                        add_square()
                        ahead(u0)
                        n["later"] = lambda: ahead(u1)
                    else:
                        ahead(u1)
                        add_square()

                for k in range(KD):
                    down(k == KD - 1)
                    if k in ADA_AT_DOWN:
                        ada_tile()
                residual_deviation()

            def run_enter(_):
                for k in range(KD):
                    v.scalar_tensor_tensor(X[:, k, LAT], X[:, k, LAT], col("norm_final", k), ps[:, STAT, 0:S], ALU.mult, ALU.mult
                                           ).then_inc(x_final if n["last"] else x_norm, 1)
                if n["last"]:
                    return
                n["norm"] += KD
                dve.wait_ge(ctx_loaded, 16)
                step(v.tensor_tensor(mod[:, :, :], mod[:, :, :], col("ada_b", 0, MOD_TILES).unsqueeze(2).to_broadcast([P, MOD_TILES, 2]),
                                     ALU.add))
                sync()
                for layer in range(2):
                    for chunk in (1, 4):
                        j = (layer * ADA_CHUNKS + chunk) * KD
                        step(v.tensor_scalar(mod[:, j:j + KD, :], mod[:, j:j + KD, :], 1.0, None, ALU.add))
                sync()
                dve.wait_ge(x_norm, n["norm"])
                modulate(0, 0, ALL)
                later()

            def rope(dst, made, done):
                turned = p_ring[:, 0, 0:S]
                bank = ready(made)
                v.tensor_tensor(turned, ps[:, bank, LAT], col("sin", 0, S), ALU.mult).then_inc(taken["D"], 1)
                step(v.tensor_tensor(dst[:, LAT], dst[:, LAT], col("cos", 0, S), ALU.mult))
                sync()
                dve.wait_ge(taken["D"], made[1].c + 1)
                v.tensor_tensor(dst[:, LAT], dst[:, LAT], turned, ALU.add).then_inc(rope_ready, 1)
                dve.wait_ge(rope_ready, done)

            def run_mla(_):
                scale_residual(ALL)
                skip("AA", 3)

                def compressed_norm(raw, gain, nk, hi, lo):
                    reciprocal_deviation(2 * S)
                    operand_tiles(nk, lambda k, t: v.scalar_tensor_tensor(t, raw[:, k, :], col(gain, k), rstd, ALU.mult, ALU.mult),
                                  lambda k: hi[:, k, :], lambda k: lo[:, k, :], 2 * S)

                compressed_norm(cq_raw, "q_norm", QR, cq_hi, cq_lo)
                u, made = next_unit("AD")
                dve.wait_ge(operand, n["tile"])
                dve.wait_ge(taken["A"], cnt.n["A"])
                rope(pe_sb[:, 4, :], made[1], 1)
                ahead(u)
                compressed_norm(ckv_raw, "kv_norm", KR, ckv_hi, ckv_lo)
                skip("AAAA", 3)
                a_end = cnt.n["A"]
                u, made = next_unit("DDDD")
                for m in range(4):
                    dve.wait_ge(taken["A"], a_end - 4 + m + 1)
                    rope(pe_sb[:, m, :], made[m], m + 2)
                ahead(u)
                skip("A" * 8)
                u, made = next_unit("D" * 8)
                for i, m in enumerate(made):
                    bank = ready(m)
                    tt, c = divmod(i, 2)
                    v.tensor_copy(v_sb[:, tt, 512 * c:512 * c + 512], ps[:, bank, :]).then_inc(taken["D"], 1)
                ahead(u)
                attention("mla0")
                gated_residual_units(0, 2, ALL)
                layer_norm(ALL, 2 * S, "ln1_g", "ln1_b", 0, (0, 3, ALL, ALL))

            def run_mlp(i):
                cols, T = (ALL, 2 * S) if i == 0 else (LAT, S)
                for k in range(KD):
                    ins = v.memset(y_acc[:, k, 0:T], 0.0)
                    if i == 0 and k < 2:
                        ins.then_inc(hid_f, 1)
                    else:
                        step(ins)
                sync()
                if i == 0:
                    dve.wait_ge(hid_f, 2)

                def quarter():
                    for q in range(4):
                        u, made = next_unit("AA")
                        for m in range(2):
                            wait(dve, taken["A"], made[m][1] + 1)
                            k = 2 * q + m
                            r, h = cnt.next("relu"), cnt.next("hid")
                            y = t_ring[:, r.odd, 0:T]
                            x = p_ring[:, made[m][1].odd, 0:T]
                            v.tensor_tensor(y, x, x, ALU.mult).then_inc(hid_f, 1)
                            wait(dve, hid_f, r + 1)
                            v.tensor_copy(mlp_hi[:, k, 0:T], y).then_inc(hid_h, 1)
                            wait(dve, hid_h, h + 1)
                            minus(mlp_lo[:, k, 0:T], y, mlp_hi[:, k, 0:T]).then_inc(hid_ready, 1)
                        ahead(u)
                        wait(dve, hid_ready, h + 1)
                    for q in range(4):
                        u, made = next_unit("DD")
                        for m in range(2):
                            bank = ready(made[m])
                            k = 2 * q + m
                            v.tensor_tensor(y_acc[:, k, 0:T], ps[:, bank, 0:T], y_acc[:, k, 0:T], ALU.add).then_inc(taken["D"], 1)
                        ahead(u)

                with cnt.loop(dve, 3, unit=8, A=8, D=8, mid=8, relu=8, hid=8):
                    quarter()
                quarter()
                dve.wait_ge(taken["D"], cnt.n["D"])
                for k in range(KD):
                    for c, s_ in HALVES if i == 0 else [(LAT, 0)]:
                        y = y_acc[:, k, c] if i == 0 else y_acc[:, k, 0:S]
                        last = v.scalar_tensor_tensor(X[:, k, c], y, mods(i, 5, k, s_), X[:, k, c], ALU.mult, ALU.add)
                    last.then_inc(x_mixed, 1)
                layer_norm(cols, T, "ln2_g", "ln2_b", i, (1, 0, ALL, LAT) if i == 0 else None)

            def run_na(_):
                step(v.memset(bias_ring[:, 0:4, 0:S], 0.0))
                skip("AA", 8)
                dve.wait_ge(bv_loaded, 16)
                bv = p_ring[:, 0:2, :].rearrange("p a b -> p (a b)")
                for i in range(4):
                    values("DDDD", i * KV, KV, bv[:, i * KV:(i + 1) * KV])
                sync()
                attention("na0", bias=True)
                gated_residual_units(1, 2, LAT)
                layer_norm(LAT, S, "ln1_g", "ln1_b", 1, (1, 3, LAT, LAT))

            dve.wait_ge(small_loaded, 16)
            run = dict(nsa=run_nsa, ffn=run_ffn, moba=run_moba, conv=run_conv, enter=run_enter, mla=run_mla, mlp=run_mlp, na=run_na)
            for at, (stage_name, arg) in enumerate(PROGRAM):
                n["last"] = at == len(PROGRAM) - 1
                run[stage_name](arg)

        @block.gpsimd
        def _(pool):
            def split(u):
                c = halves(UNIT_WIDTHS[u.c])[1]
                wait(pool, hi_split, u.times(2) + 2)
                nc.gpsimd.tensor_tensor(w_lo[:, u.odd, c], stage[:, u.odd, c], w_hi[:, u.odd, c].bitcast(F32),
                                        ALU.subtract).then_inc(lo_rest, 1)

            u, period = 0, 2
            while u < U:
                times = repeats(UNIT_WIDTHS, u, period)
                if times > 1:
                    with pool.Fori(0, times) as i:
                        for r in range(period):
                            split(Num(u + r, period, i))
                    u += times * period
                else:
                    split(Num(u))
                    u += 1


def _tiles(w, kt, mt):
    m = w.shape[1] // (P * mt)
    t = w.reshape(kt, P, m, mt, P).transpose(2, 1, 3, 0, 4)
    return list(t.reshape(m, P, kt * mt * P))


def _cols(w, width):
    kt, m = w.shape[0] // P, w.shape[1] // width
    return list(w.reshape(kt, P, m, width).transpose(2, 1, 0, 3).reshape(m, P, kt * width))


def _units(i):
    cat = np.concatenate
    heads = [(2 * pair + e) * REP + r for pair in range(2) for r in range(REP) for e in range(2)]
    head_cols = np.concatenate([np.arange(h * HD, (h + 1) * HD) for h in heads])
    swap = np.arange(ROPE) ^ 16
    for stage_name, j in PROGRAM:
        if stage_name == "nsa":
            w = i["nsa_w_in"][j]
            q = HEADS * HD
            parts = [w[:, q + n * KV:q + (n + 1) * KV] for n in range(6)]
            yield from _tiles(parts[0], KD, 2)
            yield from _tiles(parts[1], KD, 2)
            yield from _tiles(w[:, head_cols], KD, 2)
            yield from _tiles(parts[2], KD, 2)
            yield from _tiles(parts[4], KD, 2)
            yield from _cols(parts[3], KV)
            yield from _cols(parts[5], KV)
            yield from _tiles(i["nsa_cmp_k_w1"][j], 16, 1)
            yield from _tiles(i["nsa_cmp_v_w1"][j], 16, 1)
            k2 = i["nsa_cmp_k_w2"][j]
            yield cat([*_tiles(cat([k2, k2], axis=1), 2, 1), *_cols(i["nsa_cmp_v_w2"][j], HD),
                       *_cols(w[:, q + 6 * KV:], 3 * HEADS)], axis=1)
            yield from _tiles(i["nsa_w_out"][j][head_cols], KD, 2)
        elif stage_name == "moba":
            w = i["moba_w_in"][j]
            yield from _tiles(w[:, 0:2 * D], KD, 2)
            yield from _cols(w[:, 2 * D:], KV)
            yield from _tiles(i["moba_w_out"][j], KD, 2)
        elif stage_name == "conv":
            w = i["conv_w_in"][j]
            c, u = w[:, D:2 * D].reshape(D, KD, 1, P), w[:, 2 * D:].reshape(D, KD, 1, P)
            yield from _tiles(cat([c, u], axis=2).reshape(D, 2 * D), KD, 2)
            yield from _tiles(w[:, 0:D], KD, 2)
            yield from _tiles(i["conv_w_out"][j], KD, 2)
        elif stage_name == "ffn":
            g, u = (i[n][j].reshape(D, FT, 1, P) for n in ("ffn_w_gate", "ffn_w_up"))
            yield from _tiles(cat([g, u], axis=2).reshape(D, 2 * D_FF), KD, 2)
            w = i["ffn_w_down"][j].reshape(2, HALF_FT, P, KD, P).transpose(3, 0, 2, 1, 4)
            yield from w.reshape(2 * KD, P, HALF_FT * P)
        elif stage_name == "mla":
            yield from _tiles(i["mla_w_dq_2"][0], KD, 2)
            w = i["mla_w_dkv_2"][0]
            pe = w[:, KV_RANK:]
            yield from _tiles(w[:, 0:KV_RANK], KD, 2)
            yield from _tiles(cat([pe, pe, pe[:, swap], pe[:, swap]], axis=1), KD, 2)
            w = i["mla_w_uq_2"][0].reshape(Q_RANK, MLA_H, NOPE + ROPE)
            pe = w[:, :, NOPE:]
            yield from _tiles(w[:, :, 0:NOPE].reshape(Q_RANK, -1), QR, 4)
            yield from _tiles(pe.reshape(Q_RANK, -1), QR, 4)
            yield from _tiles(pe[:, :, swap].reshape(Q_RANK, -1), QR, 4)
            w = i["mla_w_ukv_2"][0].reshape(KV_RANK, MLA_H, NOPE + MLA_V)
            yield from _tiles(w[:, :, 0:NOPE].reshape(KV_RANK, -1), KR, 8)
            yield from _cols(w[:, :, NOPE:].reshape(KV_RANK, -1), D)
            yield from _tiles(i["mla_w_o_2"][0], KD, 2)
        elif stage_name == "na":
            w = i["na_w_qkv_2"][0]
            yield from _tiles(w[:, 0:2 * D], KD, 2)
            yield from _cols(w[:, 2 * D:], KV)
            yield from _tiles(i["na_w_o_2"][0], KD, 2)
        elif stage_name == "mlp":
            up = _tiles(i["mlp_w1_2"][j], KD, 2)
            down = [u for q in range(4) for u in _tiles(i["mlp_w2_2"][j][q * D:(q + 1) * D], KD, 2)]
            for q in range(4):
                yield from up[4 * q:4 * q + 4]
                yield from down[4 * q:4 * q + 4]


def _ada_units(i):
    return np.concatenate([np.asarray(i["ada_w_2"][layer]).T for layer in range(2)]).reshape(MOD_TILES, P, D)


def _features(a):
    a = np.asarray(a)
    return a.reshape(-1, P).T


def _small(i):
    s = np.zeros((P, N_SMALL), np.float32)

    def put(name, a):
        s[:, SMALL[name]] = a

    for name, key in [("norm_mix", "norm_mix"), ("norm_ffn", "norm_ffn"), ("norm_final", "norm_final"), ("ada_b", "ada_b_2"),
                      ("ln1_g", "ln1_g_2"), ("ln1_b", "ln1_b_2"), ("ln2_g", "ln2_g_2"), ("ln2_b", "ln2_b_2"),
                      ("q_norm", "mla_q_norm_2"), ("kv_norm", "mla_kv_norm_2"), ("conv_w", "conv_w")]:
        put(name, _features(i[key]))
    b = np.asarray(i["na_b_qkv_2"][0])
    put("na_bq", _features(b[0:D]))
    put("na_bk", _features(b[D:2 * D]))
    pos = np.stack([i["nsa_cmp_pos_k"], i["nsa_cmp_pos_v"]], axis=1)
    put("pos", pos.reshape(2, 2, CMP_BLOCK // 2, 2 * HD).transpose(3, 0, 1, 2).reshape(P, -1))
    put("rms_eps", RMS_EPS)
    put("ln_eps", LN_EPS)
    q = np.arange(P)[:, None] + P * np.arange(2)[None, :]
    put("valid", q >= CMP_BLOCK - 1)
    c = np.arange(CS)
    seen = (c * CMP_STRIDE + CMP_BLOCK - 1 <= q[:, :, None]) & (c < N_CMP)
    put("cmp_mask", np.where(seen, 0.0, NEG).reshape(P, -1))
    p = np.arange(P)
    put("causal", np.concatenate([np.zeros((P, P)), np.where(p[None, :] <= p[:, None], 0.0, NEG)], axis=1))
    put("ident", np.eye(P))
    put("ones", 1.0)
    d = p % ROPE
    t = np.arange(S)
    pos = np.where((d < ROPE // 2)[:, None], t // GRID_W, t % GRID_W).astype(np.float32)
    n = ROPE // 4
    freqs = np.power(np.float32(ROPE_THETA), -(np.arange(n, dtype=np.float32) / np.float32(n))).astype(np.float32)
    ang = pos * freqs[d % n][:, None]
    put("cos", np.cos(ang))
    put("sin", np.sin(ang) * np.where(d % (2 * n) < n, -1.0, 1.0)[:, None].astype(np.float32))
    return s


def _na_bias(rpb):
    t = np.arange(S)
    r, c = t // GRID_W, t % GRID_W
    start = np.clip(c - NA_COLS // 2, 0, GRID_W - NA_COLS)
    seen = (c[None, :] >= start[:, None]) & (c[None, :] < start[:, None] + NA_COLS)
    dr = r[None, :] - r[:, None] + NA_ROWS - 1
    dc = np.clip(c[None, :] - c[:, None] + NA_COLS - 1, 0, 2 * NA_COLS - 2)
    bias = np.asarray(rpb)[:, dr, dc]
    bias[:, ~seen] = NEG
    return bias.reshape(HEADS, 2, P, S)


def kernel(**inputs):
    import concourse.bacc as bacc
    from concourse.bass_utils import run_bass_kernel_spmd as run

    i = {k: np.asarray(a) for k, a in inputs.items()}
    units, ada_units = _units(i), iter(_ada_units(i))
    weights = np.zeros((P, len(STREAM), UC), np.float32)
    for at, (kind, _) in enumerate(STREAM):
        part = next(units if kind == "weights" else ada_units)
        assert part.shape == (P, STREAM_WIDTHS[at]), (at, part.shape)
        weights[:, at, 0:part.shape[1]] = part
    arrays = {
        "weights": weights.reshape(P, len(STREAM) * UC),
        "small": _small(i),
        "x_t": np.ascontiguousarray(i["x"][0].T),
        "c_rows": np.ascontiguousarray(np.broadcast_to(np.stack([i["c_2"][0], i["c_ctx_2"]]), (P, 2, D))),
        "ctx_t": np.ascontiguousarray(i["ctx_2"][0].T),
        "na_bias": np.ascontiguousarray(_na_bias(i["na_rpb_2"][0])),
        "na_bv": np.ascontiguousarray(np.broadcast_to(i["na_b_qkv_2"][0][2 * D:], (P, D))),
    }
    nc = bacc.Bacc("TRN2", target_bir_lowering=False, num_devices=1, dynamic_dma_scratch_size=1024)
    args = [nc.dram_tensor(name, a.shape, F32, kind="ExternalInput").ap() for name, a in arrays.items()]
    out = nc.dram_tensor("out_t", (D, S), F32, kind="ExternalOutput").ap()
    program(nc, *args, out)
    got = run(nc, [arrays], core_ids=[0])
    return np.ascontiguousarray(got.results[0]["out_t"].T).reshape(1, S, D)
```
